# Optimizing a Trainium2 kernel written in Bass

```python
import math
import jax, jax.numpy as jnp
from jax import lax
import numpy as np

D_MODEL = 4096
BATCH = 1
SEQ = 256
DEPTH = 1

HEAD_DIM = 128
N_HEADS_A = D_MODEL // (2 * HEAD_DIM)
N_KV_A = N_HEADS_A // 4
GROUP_A = N_HEADS_A // N_KV_A
N_HEADS_B = D_MODEL // (2 * HEAD_DIM)
CMP_LEN = 32
CMP_STRIDE = 16
CMP_HIDDEN = 256
SEL_LEN = 64
TOP_N = 16
WIN = 512
DILATIONS = ((128, 1), (512, 4), (2048, 16))
BLK = 128
SEL_CHUNK = 32
ROPE_THETA = 10000.0
EPS = 1e-6
FORCE_BONUS = 1e4
NEG = -1e30
C_IN = (2 * N_HEADS_A * HEAD_DIM + 3 * N_HEADS_A + 6 * N_KV_A * HEAD_DIM
        + 4 * N_HEADS_B * HEAD_DIM)

kernel_name = "hymba_nsa_dilated_hybrid_block"

def rms_norm(x, w):
    xf = x.astype(jnp.float32)
    y = xf * lax.rsqrt(jnp.mean(xf * xf, axis=-1, keepdims=True) + EPS)
    return (y * w.astype(jnp.float32)).astype(x.dtype)

def rope(x, pos):
    half = x.shape[-1] // 2
    inv = ROPE_THETA ** (-jnp.arange(half, dtype=jnp.float32) / half)
    ang = pos.astype(jnp.float32)[:, None, :, None] * inv
    cos, sin = jnp.cos(ang), jnp.sin(ang)
    x1 = x[..., :half].astype(jnp.float32)
    x2 = x[..., half:].astype(jnp.float32)
    return jnp.concatenate([x1 * cos - x2 * sin, x2 * cos + x1 * sin], axis=-1).astype(x.dtype)

def to_heads(t, h):
    b, s, _ = t.shape
    return t.reshape(b, s, h, HEAD_DIM).transpose(0, 2, 1, 3)

def band_attention(q, k, v, max_dist):
    n, hk, g, L, dh = q.shape
    nb = -(-L // BLK)
    lp = nb * BLK
    npv = -(-max_dist // BLK)
    kb_len = (npv + 1) * BLK
    qb = jnp.pad(q, ((0, 0), (0, 0), (0, 0), (0, lp - L), (0, 0))).reshape(n, hk, g, nb, BLK, dh)
    pad_kv = ((0, 0), (0, 0), (npv * BLK, lp - L), (0, 0))
    kp = jnp.pad(k, pad_kv)
    vp = jnp.pad(v, pad_kv)

    def blocks(t):
        return jnp.concatenate(
            [t[:, :, o * BLK:(o + nb) * BLK].reshape(n, hk, nb, BLK, dh) for o in range(npv + 1)], axis=3)

    kb, vb = blocks(kp), blocks(vp)
    s = jnp.einsum('nhgiqd,nhikd->nhgiqk', qb, kb).astype(jnp.float32)
    blk_i = jnp.arange(nb)
    qpos = (blk_i[:, None] * BLK + jnp.arange(BLK)[None, :])[:, :, None]
    kpos = ((blk_i - npv)[:, None] * BLK + jnp.arange(kb_len)[None, :])[:, None, :]
    dist = qpos - kpos
    mask = (dist >= 0) & (dist <= max_dist) & (kpos >= 0)
    s = jnp.where(mask, s, NEG)
    m = jnp.max(s, axis=-1)
    p = jnp.exp(s - m[..., None])
    den = jnp.sum(p, axis=-1)
    num = jnp.einsum('nhgiqk,nhikd->nhgiqd', p, vb.astype(jnp.float32))
    num = num.reshape(n, hk, g, lp, dh)[:, :, :, :L]
    m = m.reshape(n, hk, g, lp)[..., :L]
    den = den.reshape(n, hk, g, lp)[..., :L]
    return num, m, den

def compress(k, pe, w1, w2):
    b, hk, s, dh = k.shape
    r = CMP_LEN // CMP_STRIDE
    nchunk = s // CMP_STRIDE
    kc = k.reshape(b, hk, nchunk, CMP_STRIDE, dh)
    n_c = nchunk - r + 1
    blk = jnp.concatenate([kc[:, :, o:o + n_c] for o in range(r)], axis=3) + pe
    flat = blk.reshape(b, hk, n_c, CMP_LEN * dh)
    return jax.nn.gelu(flat @ w1) @ w2

def nsa_mixer(q, k_cmp, v_cmp, k_slc, v_slc, k_win, v_win, gates, pos,
              pe_k, pe_v, wk1, wk2, wv1, wv2):
    b, _, s_len, dh = q.shape
    scale = dh ** -0.5
    t = jnp.arange(s_len)
    q_raw = q.reshape(b, N_KV_A, GROUP_A, s_len, dh) * scale
    q_rot = rope(q, pos).reshape(b, N_KV_A, GROUP_A, s_len, dh) * scale

    kc = compress(k_cmp, pe_k, wk1, wk2)
    vc = compress(v_cmp, pe_v, wv1, wv2)
    n_c = kc.shape[2]
    sc = jnp.einsum('bhgtd,bhcd->bhgtc', q_raw, kc).astype(jnp.float32)
    c_end = jnp.arange(n_c) * CMP_STRIDE + CMP_LEN - 1
    c_valid = c_end[None, :] <= t[:, None]
    p_cmp = jax.nn.softmax(jnp.where(c_valid, sc, NEG), axis=-1) * c_valid.any(-1)[:, None]
    o_cmp = jnp.einsum('bhgtc,bhcd->bhgtd', p_cmp, vc.astype(jnp.float32))

    n_sel = s_len // SEL_LEN
    k_top = min(TOP_N, n_sel)
    ci = jnp.arange(n_c) * CMP_STRIDE
    sj = jnp.arange(n_sel) * SEL_LEN
    overlap = ((ci[:, None] < sj[None, :] + SEL_LEN) & (ci[:, None] + CMP_LEN > sj[None, :])).astype(jnp.float32)
    imp = jnp.einsum('bhgtc,cj->bhtj', p_cmp, overlap)
    cur = t // SEL_LEN
    jj = jnp.arange(n_sel)[None, :]
    forced = (jj == 0) | (jj == cur[:, None]) | (jj == cur[:, None] - 1)
    imp = jnp.where(forced, imp + FORCE_BONUS, imp)
    imp = jnp.where(sj[None, :] <= t[:, None], imp, -jnp.inf)
    _, idx = lax.top_k(imp, k_top)

    ks = rope(k_slc, pos).reshape(b, N_KV_A, n_sel, SEL_LEN, dh)
    vs = v_slc.reshape(b, N_KV_A, n_sel, SEL_LEN, dh)
    bi = jnp.arange(b)[:, None, None, None]
    hi = jnp.arange(N_KV_A)[None, :, None, None]
    nch = s_len // SEL_CHUNK

    def sel_chunk(args):
        qc, ic, tc = args
        kg = ks[bi, hi, ic].reshape(b, N_KV_A, SEL_CHUNK, k_top * SEL_LEN, dh)
        vg = vs[bi, hi, ic].reshape(b, N_KV_A, SEL_CHUNK, k_top * SEL_LEN, dh)
        kpos = (ic[..., None] * SEL_LEN + jnp.arange(SEL_LEN)).reshape(b, N_KV_A, SEL_CHUNK, k_top * SEL_LEN)
        mask = kpos <= tc[None, None, :, None]
        sc_ = jnp.einsum('bhgcd,bhckd->bhgck', qc, kg).astype(jnp.float32)
        p = jax.nn.softmax(jnp.where(mask[:, :, None], sc_, NEG), axis=-1)
        return jnp.einsum('bhgck,bhckd->bhgcd', p, vg.astype(jnp.float32))

    q_chunks = q_rot.reshape(b, N_KV_A, GROUP_A, nch, SEL_CHUNK, dh).transpose(3, 0, 1, 2, 4, 5)
    i_chunks = idx.reshape(b, N_KV_A, nch, SEL_CHUNK, k_top).transpose(2, 0, 1, 3, 4)
    t_chunks = t.reshape(nch, SEL_CHUNK)
    o_slc = lax.map(sel_chunk, (q_chunks, i_chunks, t_chunks))
    o_slc = o_slc.transpose(1, 2, 3, 0, 4, 5).reshape(b, N_KV_A, GROUP_A, s_len, dh)

    num, _, den = band_attention(q_rot, rope(k_win, pos), v_win, WIN - 1)
    o_win = num / den[..., None]

    o = gates[..., 0:1] * o_cmp + gates[..., 1:2] * o_slc + gates[..., 2:3] * o_win
    return o.reshape(b, N_HEADS_A, s_len, dh)

def dilated_mixer(q, k, v, pos):
    b, h, s_len, dh = q.shape
    q = rope(q, pos) * (dh ** -0.5)
    k = rope(k, pos)
    nums, ms, dens = [], [], []
    for window, d in DILATIONS:
        L = s_len // d

        def to_sub(t):
            return t.reshape(b, h, L, d, dh).transpose(0, 3, 1, 2, 4).reshape(b * d, h, L, dh)

        num, m, den = band_attention(to_sub(q)[:, :, None], to_sub(k), to_sub(v), window // d)
        nums.append(num.reshape(b, d, h, L, dh).transpose(0, 2, 3, 1, 4).reshape(b, h, s_len, dh))
        ms.append(m.reshape(b, d, h, L).transpose(0, 2, 3, 1).reshape(b, h, s_len))
        dens.append(den.reshape(b, d, h, L).transpose(0, 2, 3, 1).reshape(b, h, s_len))
    ms = jnp.stack(ms)
    w = jnp.exp(ms - jnp.max(ms, axis=0, keepdims=True))
    numer = jnp.sum(w[..., None] * jnp.stack(nums), axis=0)
    denom = jnp.sum(w * jnp.stack(dens), axis=0)
    return numer / denom[..., None]

def setup_inputs(seed: int = 0) -> dict:
    key = jax.random.key(seed)
    ks = jax.random.split(key, 14)
    f32 = jnp.float32
    x = jax.random.normal(ks[0], (BATCH, SEQ, D_MODEL), f32)
    offset = jax.random.randint(ks[1], (BATCH, 1), 0, 1024, dtype=jnp.int32)
    positions = (offset + jnp.arange(SEQ, dtype=jnp.int32)[None, :]).astype(jnp.int32)
    pre_norm_w = 1.0 + 0.05 * jax.random.normal(ks[2], (DEPTH, D_MODEL), f32)
    post_norm_w = 1.0 + 0.05 * jax.random.normal(ks[3], (DEPTH, D_MODEL), f32)
    w_in = jax.random.normal(ks[4], (DEPTH, D_MODEL, C_IN), f32) * D_MODEL ** -0.5
    b_gate = 0.01 * jax.random.normal(ks[5], (DEPTH, 3 * N_HEADS_A), f32)
    cmp_pe_k = 0.1 * jax.random.normal(ks[6], (DEPTH, CMP_LEN, HEAD_DIM), f32)
    cmp_pe_v = 0.1 * jax.random.normal(ks[7], (DEPTH, CMP_LEN, HEAD_DIM), f32)
    cmp_wk1 = jax.random.normal(ks[8], (DEPTH, CMP_LEN * HEAD_DIM, CMP_HIDDEN), f32) * (CMP_LEN * HEAD_DIM) ** -0.5
    cmp_wk2 = jax.random.normal(ks[9], (DEPTH, CMP_HIDDEN, HEAD_DIM), f32) * CMP_HIDDEN ** -0.5
    cmp_wv1 = jax.random.normal(ks[10], (DEPTH, CMP_LEN * HEAD_DIM, CMP_HIDDEN), f32) * (CMP_LEN * HEAD_DIM) ** -0.5
    cmp_wv2 = jax.random.normal(ks[11], (DEPTH, CMP_HIDDEN, HEAD_DIM), f32) * CMP_HIDDEN ** -0.5
    mix_width = (N_HEADS_A + N_HEADS_B) * HEAD_DIM
    w_out = jax.random.normal(ks[12], (DEPTH, mix_width, D_MODEL), f32) * mix_width ** -0.5
    return {"x": x, "positions": positions, "pre_norm_w": pre_norm_w, "post_norm_w": post_norm_w,
            "w_in": w_in, "b_gate": b_gate, "cmp_pe_k": cmp_pe_k, "cmp_pe_v": cmp_pe_v,
            "cmp_wk1": cmp_wk1, "cmp_wk2": cmp_wk2, "cmp_wv1": cmp_wv1, "cmp_wv2": cmp_wv2,
            "w_out": w_out}

def reference(x, positions, pre_norm_w, post_norm_w, w_in, b_gate, cmp_pe_k, cmp_pe_v,
              cmp_wk1, cmp_wk2, cmp_wv1, cmp_wv2, w_out):
    b, s_len, _ = x.shape
    wa = N_HEADS_A * HEAD_DIM
    wkv = N_KV_A * HEAD_DIM
    wb = N_HEADS_B * HEAD_DIM
    sizes = [wa, wa, 3 * N_HEADS_A, wkv, wkv, wkv, wkv, wkv, wkv, wb, wb, wb, wb]
    splits = [int(v) for v in np.cumsum(sizes)[:-1]]
    for l in range(DEPTH):
        h = rms_norm(x, pre_norm_w[l])
        proj = h @ w_in[l]
        qa, za, ga, kc, vc, ksl, vsl, kw, vw, qb, kb, vb, zb = jnp.split(proj, splits, axis=-1)
        gates = jax.nn.sigmoid((ga + b_gate[l]).astype(jnp.float32))
        gates = gates.reshape(b, s_len, N_HEADS_A, 3).transpose(0, 2, 1, 3).reshape(b, N_KV_A, GROUP_A, s_len, 3)
        oa = nsa_mixer(to_heads(qa, N_HEADS_A), to_heads(kc, N_KV_A), to_heads(vc, N_KV_A),
                       to_heads(ksl, N_KV_A), to_heads(vsl, N_KV_A), to_heads(kw, N_KV_A),
                       to_heads(vw, N_KV_A), gates, positions,
                       cmp_pe_k[l], cmp_pe_v[l], cmp_wk1[l], cmp_wk2[l], cmp_wv1[l], cmp_wv2[l])
        ob = dilated_mixer(to_heads(qb, N_HEADS_B), to_heads(kb, N_HEADS_B), to_heads(vb, N_HEADS_B), positions)
        oa = oa.transpose(0, 2, 1, 3).reshape(b, s_len, wa)
        ob = ob.transpose(0, 2, 1, 3).reshape(b, s_len, wb)
        mix = jnp.concatenate([oa * jax.nn.silu(za.astype(jnp.float32)),
                               ob * jax.nn.silu(zb.astype(jnp.float32))], axis=-1).astype(x.dtype)
        x = x + rms_norm(mix @ w_out[l], post_norm_w[l])
    return x


_drawn_inputs = setup_inputs


def setup_inputs(seed=0):
    import zlib

    import numpy as np

    out = dict(_drawn_inputs(seed))
    spreads = {}
    factors = {'b_gate': 25.285, 'cmp_pe_k': 4.866}
    for name, (base, spread) in spreads.items():
        noise = np.random.default_rng([zlib.crc32(name.encode()), seed]).standard_normal(out[name].shape)
        drawn = base * np.exp(spread * noise) if base else spread * noise
        out[name] = __import__('jax').numpy.asarray(drawn.astype(out[name].dtype))
    for name, factor in factors.items():
        out[name] = (out[name] * factor).astype(out[name].dtype)
    return out
```

```python
import math
from contextlib import ExitStack

import concourse.bass as bass
import numpy as np
from concourse import mybir
from concourse.alu_op_type import AluOpType as ALU

F32 = mybir.dt.float32
F32R = mybir.dt.float32r
I32 = mybir.dt.int32
ACT = mybir.ActivationFunctionType
AX = mybir.AxisListType

P = 128
D_MODEL, SEQ, HEAD = 4096, 256, 128
TILES = SEQ // P
KB = D_MODEL // P
PAIRS = KB // 2
NC = 512
GROUPS = 4
HPG = 4
N_HEADS = 16
N_GATE = 3 * N_HEADS
CMP_LEN, CMP_STRIDE, CMP_HIDDEN = 32, 16, 256
N_CMP = SEQ // CMP_STRIDE - 1
CMP_PAD = 16
SCALE = HEAD ** -0.5
EPS = 1e-6
NEG = -1e30
ROPE_THETA = 10000.0
RAW_SLOTS, SPLIT_SLOTS, LEAD = 4, 4, 3

_SIZES = [2048, 2048, N_GATE] + [512] * 6 + [2048] * 4
QA, ZA, GA, KC, VC, KSL, VSL, KW, VW, QB, KBC, VB, ZB = [sum(_SIZES[:i]) for i in range(13)]

C_KSL = 0
C_LOOP1 = 1
C_KW, C_GA, C_CMP, C_QA0 = 5, 6, 7, 8
C_A = 9
C_B = C_A + 2 * GROUPS - 1
C_OUT = C_B + 4 * GROUPS
N_OUT = D_MODEL // NC

FILL_KSL, FILL_KW, FILL_CMP, FILL_A = 4, 6, 8, 11
FILLS_A, FILLS_FINAL = 12, 2
FILL_B = FILL_A + GROUPS * (FILLS_A + FILLS_FINAL) - FILLS_FINAL
FILLS_B = FILLS_FINAL + 2 + 2 + 3
FILL_LAST = FILL_B + GROUPS * FILLS_B
UNITS_A, UNITS_B = 7, 3
UNIT_B = GROUPS * UNITS_A
UNITS = [(0, 0, 4), (1, 0, 2), (1, 2, 2)]
CONST_COLS = 128 + 384 + 384 + 2 * CMP_PAD + TILES + 64 + 2 * CMP_LEN + N_GATE


def build(nc, x, x_t, positions, norm_cols, consts, w_in, w1, w2, post_w, w_out, out):
    ctx = ExitStack()
    with ctx:
        at = [1152]

        def sb(name, shape, dt=F32, offset=None):
            size = 4 * math.prod(shape[1:])
            where = at[0] if offset is None else offset
            if offset is None:
                at[0] += (size + 31) // 32 * 32
            t = nc.alloc_sbuf_tensor_at(name, shape, dt, offset=where)
            return t, where

        x_hi, _ = sb("x_hi", [P, KB, SEQ], F32R)
        x_lo, _ = sb("x_lo", [P, KB, SEQ], F32R)
        mix_t, region = sb("mix_t", [P, KB, SEQ])
        xt_raw, _ = sb("xt_raw", [P, KB, SEQ], offset=region)
        flat_hi, _ = sb("flat_hi", [P, CMP_LEN, P], F32R, offset=region)
        flat_lo, _ = sb("flat_lo", [P, CMP_LEN, P], F32R, offset=region + 4 * CMP_LEN * P)
        y, _ = sb("y", [P, TILES, D_MODEL], offset=region)
        raw, _ = sb("raw", [P, RAW_SLOTS, 2, NC])
        w_hi, _ = sb("w_hi", [P, SPLIT_SLOTS, 2, NC], F32R)
        w_lo, _ = sb("w_lo", [P, SPLIT_SLOTS, 2, NC], F32R)
        k_t, late = sb("k_t", [P, 2, HPG, SEQ])
        v_tok, _ = sb("v_tok", [P, 2, TILES, NC])
        qraw_t, _ = sb("qraw_t", [P, HPG, SEQ])
        qrot_t, _ = sb("qrot_t", [P, HPG, SEQ])
        probs, p_off = sb("probs", [P, 4, NC])
        x_tok, _ = sb("x_tok", [P, TILES, D_MODEL], offset=late)
        blocks, _ = sb("blocks", [P, 2, HPG, N_CMP, CMP_STRIDE], offset=p_off)
        probs_t, _ = sb("probs_t", [P, 2, NC])
        tok_a, _ = sb("tok_a", [P, TILES, NC])
        tok_b, _ = sb("tok_b", [P, TILES, NC])
        rot, _ = sb("rot", [P, TILES, NC])
        rot_tmp, _ = sb("rot_tmp", [P, NC])
        mixed, _ = sb("mixed", [P, TILES, NC])
        wpost, _ = sb("wpost", [P, 2, NC])
        cst, _ = sb("cst", [P, CONST_COLS])
        pos_i, _ = sb("pos_i", [P, TILES], I32)
        pos_f, _ = sb("pos_f", [P, TILES])
        trig, _ = sb("trig", [P, 2, TILES, 64])
        turns, _ = sb("turns", [P, 2, TILES, 64])
        w2_sb, _ = sb("w2_sb", [P, 2, 2, P])
        hidden, _ = sb("hidden", [P, CMP_HIDDEN])
        gelu, _ = sb("gelu", [P, CMP_HIDDEN])
        hid_t, _ = sb("hid_t", [P, 2, P])
        kc_t, _ = sb("kc_t", [P, GROUPS * CMP_PAD])
        vc, _ = sb("vc", [CMP_PAD, GROUPS, HEAD])
        gates, _ = sb("gates", [P, TILES, N_HEADS, 3])
        probs_c, _ = sb("probs_c", [P, TILES, HPG, CMP_PAD])
        negmax, _ = sb("negmax", [P, 4, HPG])
        den, _ = sb("den", [P, 4, HPG])
        rden, _ = sb("rden", [P, 4, HPG])
        weight, _ = sb("weight", [P, 4, HPG])
        cstat, _ = sb("cstat", [P, 4, TILES, HPG])
        stat, _ = sb("stat", [P, 8, TILES])
        scl, _ = sb("scl", [P, 2, TILES])
        ssq, _ = sb("ssq", [P, 2, TILES])
        ssum, _ = sb("ssum", [P, TILES])
        junk, _ = sb("junk", [P, NC])
        assert at[0] <= nc.sbuf_usable_end, at[0]

        norm_w, _ = sb("norm_w", [P, KB])
        assert at[0] <= nc.sbuf_usable_end, at[0]
        col = 0

        def const(width):
            nonlocal col
            col += width
            return cst[:, col - width:col]

        ident = const(P)
        causal, dilated = const(384), const(384)
        cmp_bias = const(TILES * CMP_PAD).rearrange("p (t c) -> p t c", t=TILES)
        any_cmp = const(TILES)
        inv_freq = const(64)
        pe_t = const(2 * CMP_LEN).rearrange("p (v a b) -> p v a b", v=2, a=2)
        b_gate = const(N_GATE)

        def psum(name, shape):
            return ctx.enter_context(nc.psum_tensor(name, shape, F32))

        acc = psum("acc", [P, 2, TILES, NC])
        scores = psum("scores", [P, NC])
        trans = psum("trans", [P, NC])
        heads = psum("heads", [P, TILES, NC])

        def sem(name):
            return ctx.enter_context(nc.semaphore(name))

        raw_landed = [sem(f"raw_landed{i}") for i in range(RAW_SLOTS)]
        norm_landed = sem("norm_landed")
        consts_landed = sem("consts_landed")
        w2_landed = sem("w2_landed")
        xt_landed = [sem(f"xt_landed{i}") for i in range(8)]
        xtok_landed = [sem(f"xtok_landed{i}") for i in range(TILES)]
        xres_landed = [sem(f"xres_landed{i}") for i in range(TILES)]
        wpost_landed = [sem(f"wpost_landed{i}") for i in range(2)]
        hi_ready = sem("hi_ready")
        lo_ready = sem("lo_ready")
        weights_used = sem("weights_used")
        xhi_ready = sem("xhi_ready")
        x_ready = sem("x_ready")
        mixhi_ready = sem("mixhi_ready")
        mix_ready_pairs = sem("mix_ready_pairs")
        acc0_free = sem("acc0_free")
        acc1_free = sem("acc1_free")
        tr_done = sem("tr_done")
        tr_free = sem("tr_free")
        scores_done = sem("scores_done")
        scores_free = sem("scores_free")
        max_ready = sem("max_ready")
        exp_done = sem("exp_done")
        recip_done = sem("recip_done")
        weight_done = sem("weight_done")
        probs_ready = sem("probs_ready")
        heads_done = sem("heads_done")
        rope_muls = sem("rope_muls")
        rope_subs = sem("rope_subs")
        rope_done = sem("rope_done")
        ez_ready = sem("ez_ready")
        silu_step = sem("silu_step")
        mix_ready = sem("mix_ready")
        chain = sem("chain")
        angles_ready = sem("angles_ready")
        trig_ready = sem("trig_ready")
        sumsq_done = sem("sumsq_done")
        var_ready = sem("var_ready")
        stats_ready = sem("stats_ready")
        root_done = sem("root_done")
        flat_zeroed = sem("flat_zeroed")
        flat_step = sem("flat_step")
        gate_exp = sem("gate_exp")
        cmp_step = sem("cmp_step")
        gelu_step = sem("gelu_step")
        gelu_ready = sem("gelu_ready")
        tanh_done = sem("tanh_done")
        y_square = sem("y_square")
        y_scaled = sem("y_scaled")
        ssum_done = sem("ssum_done")
        y_added = sem("y_added")
        out_done = sem("out_done")

        block = ctx.enter_context(nc.Block())

        w_in_v = w_in.rearrange("(k p) c -> p k c", p=P)
        w1_v = w1.rearrange("(k p) c -> p k c", p=P)
        w_out_v = w_out.rearrange("(k p) c -> p k c", p=P)
        x_v = x.rearrange("(t p) d -> p t d", p=P)
        xt_v = x_t.rearrange("(k p) t -> p k t", p=P)
        out_v = out.rearrange("(t p) d -> p t d", p=P)

        def lag(v):
            return not isinstance(v, int) or v > 0

        @block.sync
        def _(sp):
            def load_pair(src, c, n, col, width=NC):
                first = sp.snap(col) if not isinstance(col, int) else col
                if lag(16 * c + n - RAW_SLOTS + 1):
                    sp.wait_ge(lo_ready, 16 * c + (n - RAW_SLOTS + 1))
                sp.dma_start(raw[:, n % RAW_SLOTS, :, 0:width],
                             src[:, 2 * n:2 * n + 2, bass.ds(first, width)]
                             ).then_inc(raw_landed[n % RAW_SLOTS], 16)

            def load_chunk(src, c, col, width=NC, start=0):
                for n in range(start, PAIRS):
                    load_pair(src, c, n, col, width)

            for n in range(RAW_SLOTS):
                load_pair(w_in_v, C_KSL, n, KSL)
            for t in range(TILES):
                sp.dma_start(x_tok[:, t, :], x_v[:, t, :]).then_inc(xtok_landed[t], 16)
            load_chunk(w_in_v, C_KSL, KSL, start=RAW_SLOTS)
            with sp.Fori(0, 2) as i:
                load_chunk(w_in_v, C_LOOP1 + 2 * i, KC + (VC - KC) * i)
                load_chunk(w_in_v, C_LOOP1 + 1 + 2 * i, VSL + (VW - VSL) * i)
            load_chunk(w_in_v, C_KW, KW)
            load_chunk(w_in_v, C_GA, GA, N_GATE)
            load_chunk(w1_v, C_CMP, 0)
            load_chunk(w_in_v, C_QA0, QA)
            with sp.Fori(0, GROUPS - 1) as g:
                load_chunk(w_in_v, C_A + 2 * g, ZA + NC * g)
                load_chunk(w_in_v, C_A + 1 + 2 * g, QA + NC + NC * g)
            load_chunk(w_in_v, C_B - 1, ZA + NC * (GROUPS - 1))
            with sp.Fori(0, GROUPS) as g:
                load_chunk(w_in_v, C_B + 4 * g, QB + NC * g)
                load_chunk(w_in_v, C_B + 1 + 4 * g, KBC + NC * g)
                load_chunk(w_in_v, C_B + 2 + 4 * g, VB + NC * g)
                load_chunk(w_in_v, C_B + 3 + 4 * g, ZB + NC * g)
            for j in range(2):
                sp.dma_start(wpost[:, j, :], post_w[0:1, j * NC:(j + 1) * NC].broadcast_to([P, NC])
                             ).then_inc(wpost_landed[j], 16)
            load_chunk(w_out_v, C_OUT, 0)
            sp.wait_ge(weights_used, PAIRS * C_OUT)
            for t in range(TILES):
                sp.dma_start(x_tok[:, t, :], x_v[:, t, :]).then_inc(xres_landed[t], 16)

            def load_post(j, c, col):
                first = sp.snap(col)
                sp.wait_ge(acc0_free, c - 1)
                sp.wait_ge(acc1_free, c - 1)
                sp.dma_start(wpost[:, j, :], post_w[0:1, bass.ds(first, NC)].broadcast_to([P, NC])
                             ).then_inc(wpost_landed[j], 16)

            load_chunk(w_out_v, C_OUT + 1, NC)
            with sp.Fori(0, (N_OUT - 2) // 2) as i:
                for j in range(2):
                    load_chunk(w_out_v, C_OUT + 2 + j + 2 * i, NC * (2 + j) + 2 * NC * i)
                    load_post(j, C_OUT + 2 + j + 2 * i, NC * (2 + j) + 2 * NC * i)
            for t in range(TILES):
                for j in range(0, 4, 2):
                    sp.wait_ge(y_added, 4 * t + j + 2)
                    sp.dma_start(out_v[:, t, j * 1024:(j + 2) * 1024], y[:, t, j * 1024:(j + 2) * 1024]
                                 ).then_inc(out_done, 16)
            sp.wait_ge(out_done, 16 * 4)

        @block.gpsimd
        def _(pool):
            pool.wait_ge(x_ready, PAIRS)
            for half in (flat_hi, flat_lo):
                pad = half[:, :, :].rearrange("p l (v c) -> p l v c", c=CMP_PAD)[:, :, :, CMP_PAD - 1:CMP_PAD]
                nc.gpsimd.memset(pad.bitcast(F32), 0.0).then_inc(flat_zeroed, 1)

            def rope(src, t, chunk, tile_no):
                pool.wait_ge(acc0_free if t == 0 else acc1_free, chunk + 1)
                s4 = src[:, t, :].rearrange("p (h x d) -> p h x d", h=HPG, x=2)
                r4 = rot[:, t, :].rearrange("p (h x d) -> p h x d", h=HPG, x=2)
                m4 = rot_tmp[:, :].rearrange("p (h x d) -> p h x d", h=HPG, x=2)
                sin = trig[:, 0, t, :].unsqueeze(1).broadcast_to([P, HPG, 64])
                cos = trig[:, 1, t, :].unsqueeze(1).unsqueeze(1).broadcast_to([P, HPG, 2, 64])
                nc.gpsimd.tensor_tensor(r4, s4, cos, ALU.mult).then_inc(rope_muls, 1)
                nc.gpsimd.tensor_tensor(m4[:, :, 0, :], s4[:, :, 1, :], sin, ALU.mult).then_inc(rope_muls, 1)
                nc.gpsimd.tensor_tensor(m4[:, :, 1, :], s4[:, :, 0, :], sin, ALU.mult).then_inc(rope_muls, 1)
                pool.wait_ge(rope_muls, 3 * tile_no + 3)
                nc.gpsimd.tensor_tensor(r4[:, :, 0, :], r4[:, :, 0, :], m4[:, :, 0, :], ALU.subtract
                                        ).then_inc(rope_subs, 1)
                nc.gpsimd.tensor_tensor(r4[:, :, 1, :], r4[:, :, 1, :], m4[:, :, 1, :], ALU.add
                                        ).then_inc(rope_done, 1)
                pool.wait_ge(rope_subs, tile_no + 1)
                pool.wait_ge(rope_done, tile_no + 1)

            pool.wait_ge(trig_ready, 1)
            for t in range(TILES):
                rope(tok_b, t, C_KSL, t)
            for t in range(TILES):
                rope(tok_a, t, C_KW, 2 + t)
            for t in range(TILES):
                rope(tok_a, t, C_QA0, 4 + t)
            with pool.Fori(0, GROUPS - 1) as g:
                for t in range(TILES):
                    rope(tok_a, t, C_A + 1 + 2 * g, 6 + t + 2 * g)
            with pool.Fori(0, GROUPS) as g:
                for j in range(2):
                    for t in range(TILES):
                        rope(tok_a, t, C_B + j + 4 * g, 12 + 2 * j + t + 4 * g)

        @block.tensor
        def _(pe):
            def gemm_pair(c, n, parity, width=NC, hi=x_hi, lo=x_lo, tiles=TILES, ready=None, wait_banks=True):
                if n == 0 and wait_banks:
                    pe.wait_ge(acc0_free, c - 1)
                    pe.wait_ge(acc1_free, c - 1)
                if ready is not None:
                    pe.wait_ge(ready, n + 1)
                pe.wait_ge(lo_ready, 16 * c + n + 1)
                s = n % SPLIT_SLOTS
                for kk in range(2):
                    k = 2 * n + kk
                    for t in range(tiles):
                        o = acc[:, parity, t, 0:width]
                        stat_hi, stat_lo = hi[:, k, t * P:(t + 1) * P], lo[:, k, t * P:(t + 1) * P]
                        nc.tensor.matmul(o, stat_hi, w_hi[:, s, kk, 0:width], start=(k == 0), stop=False)
                        nc.tensor.matmul(o, stat_hi, w_lo[:, s, kk, 0:width], start=False, stop=False)
                        last = nc.tensor.matmul(o, stat_lo, w_hi[:, s, kk, 0:width],
                                                start=False, stop=(k == KB - 1))
                last.then_inc(weights_used, 1)

            def transpose4(src, fill):
                if fill is not None:
                    pe.wait_ge(tr_free, fill)
                for b in range(4):
                    last = nc.tensor.transpose(trans[:, b * P:(b + 1) * P], src[:, b * P:(b + 1) * P], ident)
                last.then_inc(tr_done, 1)

            def rotated(t, tile_no, fill):
                pe.wait_ge(rope_done, tile_no + 1)
                transpose4(rot[:, t, :], fill)

            def unit_scores(u, unit, q_t, keys, fills):
                t, h0, nh = UNITS[u]
                pe.wait_ge(tr_free, fills)
                pe.wait_ge(scores_free, unit)
                nk = P * (t + 1)
                for i in range(nh):
                    last = nc.tensor.matmul(scores[:, i * nk:(i + 1) * nk], q_t[:, h0 + i, t * P:(t + 1) * P],
                                            keys(h0 + i, nk), start=True, stop=True)
                last.then_inc(scores_done, 1)

            def unit_transpose(slot, unit, fill):
                pe.wait_ge(probs_ready, unit + 1)
                transpose4(probs[:, slot, :], fill)

            def unit_values(u, slot, values, fill, first, last_one):
                t, h0, nh = UNITS[u]
                pe.wait_ge(tr_free, fill + 1)
                for i in range(nh):
                    for b in range(t + 1):
                        blk = i * (t + 1) + b
                        last = nc.tensor.matmul(heads[:, t, (h0 + i) * P:(h0 + i + 1) * P],
                                                probs_t[:, slot % 2, blk * P:(blk + 1) * P], values(h0 + i, b),
                                                start=(first and blk == 0), stop=(last_one and b == t),
                                                skip_group_check=True)
                return last

            def attention_a(n, c, g, fill, unit, tiles_rotated):
                if n in (1, 2):
                    t = n - 1
                    pe.wait_ge(acc0_free if t == 0 else acc1_free, c)
                    transpose4(tok_a[:, t, :], fill + t)
                if n == 3:
                    pe.wait_ge(tr_free, fill + 2)
                    for t in range(TILES):
                        for h in range(HPG):
                            o = (t * HPG + h) * CMP_PAD
                            last = nc.tensor.matmul(scores[:, o:o + CMP_PAD], qraw_t[:, h, t * P:(t + 1) * P],
                                                    kc_t[:, bass.ds(CMP_PAD * g, CMP_PAD)], start=True, stop=True)
                    last.then_inc(scores_done, 1)
                if n in (4, 5):
                    rotated(n - 4, tiles_rotated + n - 4, fill + n - 2)
                if n in (6, 7):
                    t = n - 6
                    pe.wait_ge(probs_ready, unit + 1)
                    pe.wait_ge(tr_free, fill + 4 + t)
                    for h in range(HPG):
                        last = nc.tensor.transpose(trans[0:CMP_PAD, h * P:(h + 1) * P], probs_c[:, t, h, :], ident)
                    last.then_inc(tr_done, 1)
                if n in (8, 9):
                    pe.wait_ge(tr_free, fill + n - 3)
                if 6 <= n <= 11:
                    u = n - 6
                    keys = lambda h, nk: k_t[:, u // 3, g, 0:nk]
                    unit_scores(u % 3, unit + 1 + u, qrot_t, keys, fill + 4)
                if n in (8, 9):
                    t = n - 8
                    for h in range(HPG):
                        nc.tensor.matmul(heads[:, t, h * P:(h + 1) * P], probs_t[0:CMP_PAD, t, h * P:(h + 1) * P],
                                         vc[0:CMP_PAD, g, :],
                                         start=(h == 0), stop=False, skip_group_check=True)
                if 10 <= n:
                    u = n - 10
                    values = lambda h, b: v_tok[:, u // 3, b, bass.ds(P * g, P)]
                    last = unit_values(u % 3, u, values, fill + 6 + u, False, u >= 3)
                    if n == PAIRS - 1:
                        last.then_inc(heads_done, 1)
                if 9 <= n <= 14:
                    u = n - 9
                    unit_transpose(u % 4, unit + 1 + u, fill + 6 + u)

            def attention_b(n, fill, unit):
                if n in (1, 3, 5):
                    u = (n - 1) // 2
                    unit_scores(u, unit + u, qrot_t, lambda h, nk: k_t[:, 0, h, 0:nk], fill)
                if n in (4, 6, 8):
                    u = (n - 4) // 2
                    unit_transpose(u, unit + u, fill + u)
                if n in (5, 7, 9):
                    u = (n - 5) // 2
                    last = unit_values(u, u, lambda h, b: v_tok[:, 0, b, h * P:(h + 1) * P], fill + u,
                                       u < 2, True)
                    if u == 2:
                        last.then_inc(heads_done, 1)

            def final(n, fill, tiles_mixed):
                if n in (6, 9):
                    t = (n - 6) // 3
                    pe.wait_ge(mix_ready, tiles_mixed + t + 1)
                    transpose4(mixed[:, t, :], fill + t)

            pe.wait_ge(consts_landed, 16 * 2)
            for n in range(PAIRS):
                gemm_pair(C_KSL, n, 0, ready=x_ready, wait_banks=False)
            with pe.Fori(0, 2) as i:
                for n in range(PAIRS):
                    gemm_pair(C_LOOP1 + 2 * i, n, 1, wait_banks=False)
                for n in range(PAIRS):
                    if n in (1, 2):
                        pe.wait_ge(acc0_free if n == 1 else acc1_free, 2 * i + 2)
                        transpose4(tok_a[:, n - 1, :], None if n == 1 else 2 * i + 1)
                    gemm_pair(C_LOOP1 + 1 + 2 * i, n, 0)
            for n in range(PAIRS):
                if n in (4, 5):
                    rotated(n - 4, n - 4, FILL_KSL + n - 4)
                gemm_pair(C_KW, n, 1)
            for n in range(PAIRS):
                gemm_pair(C_GA, n, 0, width=N_GATE)
            pe.wait_ge(flat_step, 2 * 6)
            for n in range(PAIRS):
                if n in (4, 5):
                    rotated(n - 4, 2 + n - 4, FILL_KW + n - 4)
                gemm_pair(C_CMP, n, 1, hi=flat_hi, lo=flat_lo, tiles=1)
            for n in range(PAIRS):
                if n == 5:
                    pe.wait_ge(gelu_ready, 1)
                    pe.wait_ge(w2_landed, 16)
                    pe.wait_ge(tr_free, FILL_CMP)
                    for j in range(2):
                        last = nc.tensor.transpose(trans[:, j * P:(j + 1) * P], gelu[:, j * P:(j + 1) * P], ident)
                    last.then_inc(tr_done, 1)
                if n == 6:
                    pe.wait_ge(tr_free, FILL_CMP + 1)
                    for j in range(2):
                        last = nc.tensor.matmul(trans[:, 0:64], w2_sb[:, 0, j, :], hid_t[:, j, 0:64],
                                                start=(j == 0), stop=(j == 1))
                    last.then_inc(tr_done, 1)
                if n == 7:
                    pe.wait_ge(tr_free, FILL_CMP + 2)
                    for h in range(GROUPS):
                        for j in range(2):
                            c0 = 64 + h * CMP_PAD
                            last = nc.tensor.matmul(trans[0:CMP_PAD, h * P:(h + 1) * P], hid_t[:, j, c0:c0 + CMP_PAD],
                                                    w2_sb[:, 1, j, :], start=(j == 0), stop=(j == 1))
                    last.then_inc(tr_done, 1)
                gemm_pair(C_QA0, n, 0)

            def attention_a_chunk(c, g, fill, unit, tiles_rotated):
                for n in range(PAIRS):
                    attention_a(n, c, g, fill, unit, tiles_rotated)
                    gemm_pair(c, n, 1)

            with pe.Fori(0, GROUPS - 1) as g:
                per = FILLS_A + FILLS_FINAL
                attention_a_chunk(C_A + 2 * g, g, FILL_A + per * g, UNITS_A * g, 4 + 2 * g)
                for n in range(PAIRS):
                    final(n, FILL_A + FILLS_A + per * g, 2 * g)
                    gemm_pair(C_A + 1 + 2 * g, n, 0)
            attention_a_chunk(C_B - 1, GROUPS - 1, FILL_B - FILLS_A, UNIT_B - UNITS_A, 4 + 2 * (GROUPS - 1))
            with pe.Fori(0, GROUPS) as g:
                fill = FILL_B + FILLS_B * g
                for n in range(PAIRS):
                    final(n, fill, 2 * (GROUPS - 1) + 2 * g)
                    gemm_pair(C_B + 4 * g, n, 0)
                for j in range(2):
                    for n in range(PAIRS):
                        if n in (4, 5):
                            rotated(n - 4, 12 + 2 * j + n - 4 + 4 * g, FILL_B + 2 + 2 * j + n - 4 + FILLS_B * g)
                        gemm_pair(C_B + 1 + j + 4 * g, n, (j + 1) % 2)
                for n in range(PAIRS):
                    attention_b(n, FILL_B + 6 + FILLS_B * g, UNIT_B + UNITS_B * g)
                    gemm_pair(C_B + 3 + 4 * g, n, 1)
            for n in range(PAIRS):
                final(n, FILL_LAST, 4 * GROUPS - 2)
                gemm_pair(C_OUT, n, 0, ready=mix_ready_pairs)
            with pe.Fori(0, (N_OUT - 2) // 2) as i:
                for j in range(2):
                    for n in range(PAIRS):
                        gemm_pair(C_OUT + 1 + j + 2 * i, n, (j + 1) % 2)
            for n in range(PAIRS):
                gemm_pair(C_OUT + N_OUT - 1, n, 1)

        @block.scalar
        def _(act):
            act.dma_start(norm_w[:, :], norm_cols).then_inc(norm_landed, 16)
            for j in range(8):
                act.dma_start(xt_raw[:, 4 * j:4 * j + 4, :], xt_v[:, 4 * j:4 * j + 4, :]
                              ).then_inc(xt_landed[j], 16)
                if j == 1:
                    act.dma_start(cst[:, :], consts).then_inc(consts_landed, 16)
                    act.dma_start(pos_i[:, :], positions).then_inc(consts_landed, 16)
            act.dma_start(w2_sb[:, :, :, :], w2).then_inc(w2_landed, 16)
            act.wait_ge(norm_landed, 16)

            def split(c, n, width=NC):
                act.wait_ge(raw_landed[n % RAW_SLOTS], 16 * (4 * c + n // RAW_SLOTS + 1))
                if lag(16 * c + n - SPLIT_SLOTS + 1):
                    act.wait_ge(weights_used, 16 * c + (n - SPLIT_SLOTS + 1))
                nc.scalar.activation(w_hi[:, n % SPLIT_SLOTS, :, 0:width], raw[:, n % RAW_SLOTS, :, 0:width],
                                     ACT.Copy).then_inc(hi_ready, 1)

            def evacuate(c, parity, dst, scale):
                act.wait_ge(weights_used, PAIRS * (c + 1))
                nc.scalar.activation(dst, acc[:, parity, 0, :], ACT.Copy, scale=scale).then_inc(acc0_free, 1)

            def take_fill(fill, dst, src=None, scale=1.0):
                act.wait_ge(tr_done, fill + 1)
                src = trans[:, :].rearrange("p (h t) -> p h t", h=HPG) if src is None else src
                nc.scalar.activation(dst, src, ACT.Copy, scale=scale).then_inc(tr_free, 1)

            def exp_unit(u, slot, unit):
                t, h0, nh = UNITS[u]
                nk = P * (t + 1)
                act.wait_ge(max_ready, unit + 1)
                for i in range(nh):
                    p = probs[:, slot, i * nk:(i + 1) * nk]
                    last = nc.scalar.activation(p, p, ACT.Exp, bias=negmax[:, slot, i:i + 1],
                                                accum_out=den[:, slot, i:i + 1])
                last.then_inc(exp_done, 1)

            def exp_z(t, c, tile_no):
                act.wait_ge(acc0_free if t == 0 else acc1_free, c)
                nc.scalar.activation(mixed[:, t, :], tok_b[:, t, :], ACT.Exp, scale=-1.0).then_inc(ez_ready, 1)

            r0, rq0 = scl[:, 0, 0:1], scl[:, 1, 0:1]

            def x_block(n):
                for k in (2 * n, 2 * n + 1):
                    act.wait_ge(xt_landed[k // 4], 16)
                    nc.scalar.activation(x_hi[:, k, :], xt_raw[:, k, :], ACT.Copy, scale=norm_w[:, k:k + 1]
                                         ).then_inc(xhi_ready, 1)

            for n in range(PAIRS + LEAD):
                if n < PAIRS:
                    x_block(n)
                split(C_KSL, n)
                if n == PAIRS - 4:
                    act.wait_ge(angles_ready, 1)
                    nc.scalar.activation(trig[:, :, :, :], trig[:, :, :, :], ACT.Sin).then_inc(trig_ready, 1)
                if n == PAIRS:
                    act.wait_ge(xtok_landed[0], 16)
                    nc.scalar.activation(x_tok[:, 0, :], x_tok[:, 0, :], ACT.Square, accum_out=stat[:, 0, 0:1]
                                         ).then_inc(sumsq_done, 1)
                if n == PAIRS + 1:
                    act.wait_ge(var_ready, 1)
                    nc.scalar.activation(stat[:, 2, :], stat[:, 1, :], ACT.Sqrt).then_inc(root_done, 1)
            act.wait_ge(stats_ready, 1)
            evacuate(C_KSL, 0, tok_b[:, 0, :], r0)
            with act.Fori(0, 2) as i:
                for n in range(LEAD, PAIRS + LEAD):
                    split(C_LOOP1 + 2 * i, n)
                evacuate(C_LOOP1 + 2 * i, 1, tok_a[:, 0, :], r0)
                for n in range(LEAD, PAIRS + LEAD):
                    split(C_LOOP1 + 1 + 2 * i, n)
            for n in range(LEAD, PAIRS + LEAD):
                if n - LEAD in (4, 5):
                    t = n - LEAD - 4
                    take_fill(FILL_KSL + t, k_t[:, 0, :, t * P:(t + 1) * P])
                split(C_KW, n, NC if n < PAIRS else N_GATE)
            evacuate(C_KW, 1, tok_a[:, 0, :], r0)
            for n in range(LEAD, PAIRS + LEAD):
                split(C_GA, n, NC if n >= PAIRS else N_GATE)
            for n in range(LEAD, PAIRS + LEAD):
                if n - LEAD in (4, 5):
                    t = n - LEAD - 4
                    take_fill(FILL_KW + t, k_t[:, 1, :, t * P:(t + 1) * P])
                split(C_CMP, n)
                if n == LEAD:
                    act.wait_ge(acc0_free, C_GA + 1)
                    act.wait_ge(acc1_free, C_GA + 1)
                    nc.scalar.activation(gates[:, :, :, :], gates[:, :, :, :], ACT.Exp, scale=-1.0
                                         ).then_inc(gate_exp, 1)
            for n in range(LEAD, PAIRS + LEAD):
                if n - LEAD == 2:
                    act.wait_ge(gelu_step, 3)
                    nc.scalar.activation(gelu[:, :], gelu[:, :], ACT.Tanh, scale=math.sqrt(2 / math.pi)
                                         ).then_inc(tanh_done, 1)
                if n - LEAD == 5:
                    take_fill(FILL_CMP, hid_t[:, :, :], trans[:, 0:2 * P].rearrange("p (j r) -> p j r", j=2), 0.5)
                if n - LEAD == 6:
                    take_fill(FILL_CMP + 1, kc_t[:, :], trans[:, 0:64])
                if n - LEAD == 7:
                    take_fill(FILL_CMP + 2, vc[:, :, :], trans[0:CMP_PAD, :].rearrange("p (h d) -> p h d", h=GROUPS))
                split(C_QA0, n)
            evacuate(C_QA0, 0, tok_a[:, 0, :], rq0)

            def attention_a_frame(c, fill, unit):
                for n in range(LEAD, PAIRS + LEAD):
                    at = n - LEAD
                    if at in (1, 2):
                        take_fill(fill + at - 1, qraw_t[:, :, (at - 1) * P:at * P])
                    if at in (4, 5):
                        take_fill(fill + at - 2, qrot_t[:, :, (at - 4) * P:(at - 3) * P])
                    if at in (6, 7):
                        take_fill(fill + at - 2, probs_t[0:CMP_PAD, at - 6, :], trans[0:CMP_PAD, :])
                    if 9 <= at <= 14:
                        take_fill(fill + at - 3, probs_t[:, (at - 9) % 2, :], trans[:, :])
                    split(c, n)
                    if at == 3:
                        act.wait_ge(max_ready, unit + 1)
                        nc.scalar.activation(probs_c[:, :, :, :], probs_c[:, :, :, :], ACT.Exp).then_inc(exp_done, 1)
                    if 6 <= at <= 11:
                        exp_unit((at - 6) % 3, (at - 6) % 4, unit + 1 + at - 6)
                evacuate(c, 1, tok_b[:, 0, :], r0)

            def mixing_frame(c, tiles_mixed):
                for n in range(LEAD, PAIRS + LEAD):
                    split(c, n)
                    if n - LEAD in (0, 1):
                        exp_z(n - LEAD, c, tiles_mixed + n - LEAD)
                evacuate(c, 0, tok_a[:, 0, :], rq0)

            with act.Fori(0, GROUPS - 1) as g:
                per = FILLS_A + FILLS_FINAL
                attention_a_frame(C_A + 2 * g, FILL_A + per * g, UNITS_A * g)
                mixing_frame(C_A + 1 + 2 * g, 2 * g)
            attention_a_frame(C_B - 1, FILL_B - FILLS_A, UNIT_B - UNITS_A)
            with act.Fori(0, GROUPS) as g:
                mixing_frame(C_B + 4 * g, 2 * (GROUPS - 1) + 2 * g)
                for j in range(2):
                    for n in range(LEAD, PAIRS + LEAD):
                        if n - LEAD in (4, 5):
                            t = n - LEAD - 4
                            dst = qrot_t if j == 0 else k_t[:, 0, :, :]
                            take_fill(FILL_B + 2 + 2 * j + t + FILLS_B * g, dst[:, :, t * P:(t + 1) * P])
                        split(C_B + 1 + j + 4 * g, n)
                    evacuate(C_B + 1 + j + 4 * g, (j + 1) % 2, tok_a[:, 0, :] if j == 0 else v_tok[:, 0, 0, :], r0)
                for n in range(LEAD, PAIRS + LEAD):
                    at = n - LEAD
                    if at in (4, 6, 8):
                        u = (at - 4) // 2
                        take_fill(FILL_B + 6 + u + FILLS_B * g, probs_t[:, u % 2, :], trans[:, :])
                    split(C_B + 3 + 4 * g, n)
                    if at in (1, 3, 5):
                        u = (at - 1) // 2
                        exp_unit(u, u, UNIT_B + u + UNITS_B * g)
                evacuate(C_B + 3 + 4 * g, 1, tok_b[:, 0, :], r0)

            def square(n, parity):
                act.wait_ge(weights_used, PAIRS * (C_OUT + n + 1))
                act.wait_ge(acc1_free, C_OUT + n)
                nc.scalar.activation(junk[:, :], acc[:, parity, 0, :], ACT.Square, accum_out=ssq[:, parity, 0:1]
                                     ).then_inc(y_square, 1)
                act.wait_ge(y_scaled, n + 1)
                act.wait_ge(y_square, n + 1)
                nc.scalar.activation(junk[:, :], acc[:, parity, 1, :], ACT.Square, accum_out=ssq[:, parity, 1:2]
                                     ).then_inc(acc1_free, 1)

            def mix_block(n):
                act.wait_ge(weights_used, PAIRS * (C_OUT - 1) + n + 1)
                act.wait_ge(tr_free, FILL_LAST + (2 if n >= PAIRS - 2 else 0))
                nc.scalar.activation(x_hi[:, 2 * n:2 * n + 2, :], mix_t[:, 2 * n:2 * n + 2, :], ACT.Copy
                                     ).then_inc(mixhi_ready, 1)

            for n in range(LEAD):
                mix_block(n)
            for n in range(LEAD, PAIRS + LEAD):
                if n < PAIRS:
                    mix_block(n)
                split(C_OUT, n)
                if n - LEAD in (0, 1):
                    exp_z(n - LEAD, C_OUT, 4 * GROUPS - 2 + n - LEAD)
            square(0, 0)
            with act.Fori(0, (N_OUT - 2) // 2) as i:
                for j in range(2):
                    for n in range(LEAD, PAIRS + LEAD):
                        split(C_OUT + 1 + j + 2 * i, n)
                    square(1 + j + 2 * i, (j + 1) % 2)
            for n in range(LEAD, PAIRS):
                split(C_OUT + N_OUT - 1, n)
            square(N_OUT - 1, 1)
            act.wait_ge(var_ready, 2)
            nc.scalar.activation(stat[:, 2, :], stat[:, 1, :], ACT.Sqrt).then_inc(root_done, 1)

        @block.vector
        def _(dve):
            V = nc.vector
            links = [0]

            def link(ins):
                links[0] += 1
                ins.then_inc(chain, 1)
                dve.wait_ge(chain, links[0])

            def split(c, n, width=NC):
                dve.wait_ge(hi_ready, 16 * c + n + 1)
                s = n % SPLIT_SLOTS
                V.tensor_tensor(w_lo[:, s, :, 0:width], raw[:, n % RAW_SLOTS, :, 0:width],
                                w_hi[:, s, :, 0:width].bitcast(F32), ALU.subtract).then_inc(lo_ready, 1)

            def evacuate(c, parity, dst, scale, t=1):
                dve.wait_ge(weights_used, PAIRS * (c + 1))
                V.tensor_scalar(dst, acc[:, parity, t, :], scale, None, ALU.mult
                                ).then_inc(acc0_free if t == 0 else acc1_free, 1)

            def take_fill(fill, dst):
                dve.wait_ge(tr_done, fill + 1)
                V.tensor_scalar(dst, trans[:, :].rearrange("p (h t) -> p h t", h=HPG), 1.0, None, ALU.mult
                                ).then_inc(tr_free, 1)

            def variance():
                V.tensor_scalar(stat[:, 1, :], stat[:, 0, :], 1.0 / D_MODEL, EPS, ALU.mult, ALU.add
                                ).then_inc(var_ready, 1)

            def inverse_rms(which):
                dve.wait_ge(root_done, which)
                link(V.reciprocal(stat[:, 3, :], stat[:, 2, :]))
                link(V.tensor_tensor(stat[:, 4, :], stat[:, 3, :], stat[:, 3, :], ALU.mult))
                link(V.tensor_tensor(stat[:, 4, :], stat[:, 4, :], stat[:, 1, :], ALU.mult))
                link(V.tensor_scalar(stat[:, 4, :], stat[:, 4, :], -0.5, 1.5, ALU.mult, ALU.add))
                link(V.tensor_tensor(scl[:, 0, :], stat[:, 3, :], stat[:, 4, :], ALU.mult))

            r = [scl[:, 0, t:t + 1] for t in range(TILES)]
            rq1 = scl[:, 1, 1:2]

            def x_rest(n):
                for k in (2 * n, 2 * n + 1):
                    dve.wait_ge(xhi_ready, k + 1)
                    last = V.scalar_tensor_tensor(x_lo[:, k, :], xt_raw[:, k, :], norm_w[:, k:k + 1],
                                                  x_hi[:, k, :].bitcast(F32), ALU.mult, ALU.subtract)
                last.then_inc(x_ready, 1)

            turn_parts, rest = [], 2 * math.pi
            for bits in (5, 14, 23):
                turn_parts.append(round(rest * 2 ** bits) / 2 ** bits)
                rest -= turn_parts[-1]
            turn_parts.append(rest)

            def angles(step):
                if step == 0:
                    link(V.tensor_copy(pos_f[:, :], pos_i[:, :]))
                if step in (1, 2):
                    for t in range(TILES):
                        link(V.tensor_scalar(trig[:, step - 1, t, :], inv_freq, pos_f[:, t:t + 1], None, ALU.mult))
                if step == 3:
                    link(V.tensor_scalar(turns[:, 0, :, :], trig[:, 0, :, :], 1 / (2 * math.pi), None, ALU.mult))
                    link(V.tensor_scalar(turns[:, 1, :, :], trig[:, 1, :, :], 1 / (2 * math.pi), 0.25,
                                         ALU.mult, ALU.add))
                if step == 4:
                    link(V.tensor_scalar(turns[:, :, :, :], turns[:, :, :, :], 1.5 * 2 ** 23, None, ALU.add))
                    link(V.tensor_scalar(turns[:, :, :, :], turns[:, :, :, :], 1.5 * 2 ** 23, None, ALU.subtract))
                if step in (5, 6, 7, 8):
                    link(V.scalar_tensor_tensor(trig[:, :, :, :], turns[:, :, :, :], -turn_parts[step - 5],
                                                trig[:, :, :, :], ALU.mult, ALU.add))
                if step == 9:
                    link(V.tensor_scalar(trig[:, 1, :, :], trig[:, 1, :, :], math.pi / 2, None, ALU.add))
                    V.tensor_scalar(trig[:, :, :, :], trig[:, :, :, :], 3.1415925, -3.1415925, ALU.min, ALU.max
                                    ).then_inc(angles_ready, 1)

            dve.wait_ge(norm_landed, 16)
            for n in range(PAIRS + LEAD):
                if n < PAIRS:
                    x_rest(n)
                split(C_KSL, n)
                if n == 2:
                    dve.wait_ge(consts_landed, 16 * 2)
                angles(n - 2)
                if n == PAIRS:
                    dve.wait_ge(xtok_landed[1], 16)
                    link(V.tensor_tensor_reduce(out=x_tok[:, 1, :], in0=x_tok[:, 1, :], in1=x_tok[:, 1, :], scale=1.0,
                                                scalar=0.0, op0=ALU.mult, op1=ALU.add, accum_out=stat[:, 0, 1:2]))
                    dve.wait_ge(sumsq_done, 1)
                    variance()
            inverse_rms(1)
            V.tensor_scalar(scl[:, 1, :], scl[:, 0, :], SCALE, None, ALU.mult).then_inc(stats_ready, 1)
            dve.wait_ge(stats_ready, 1)
            evacuate(C_KSL, 0, tok_b[:, 1, :], r[1])
            dve.wait_ge(flat_zeroed, 2)

            with dve.Fori(0, 2) as i:
                for n in range(LEAD, PAIRS + LEAD):
                    split(C_LOOP1 + 2 * i, n)
                evacuate(C_LOOP1 + 2 * i, 1, tok_a[:, 1, :], r[1])
                for n in range(LEAD, PAIRS + LEAD):
                    split(C_LOOP1 + 1 + 2 * i, n)
                    at = n - LEAD
                    if at in (1, 2):
                        take_fill(2 * i + at - 1, k_t[:, i, :, (at - 1) * P:at * P])
                    if at in (4, 5):
                        a = at - 4
                        dve.wait_ge(tr_free, 2 * i + 2)
                        src = k_t[:, i, :, :].rearrange("p h (c b) -> p h c b", b=CMP_STRIDE)[:, :, a:a + N_CMP, :]
                        pe_row = pe_t[:, i, a, :].unsqueeze(1).unsqueeze(1).broadcast_to([P, HPG, N_CMP, CMP_STRIDE])
                        V.tensor_tensor(blocks[:, a, :, :, :], src, pe_row, ALU.add).then_inc(flat_step, 1)
                    if at in (6, 7, 8, 9):
                        a = at % 2
                        half = [f[:, a * CMP_STRIDE:(a + 1) * CMP_STRIDE, :].rearrange(
                            "p b (v h c) -> p v h c b", v=2, h=HPG)[:, i, :, 0:N_CMP, :] for f in (flat_hi, flat_lo)]
                        if at < 8:
                            dve.wait_ge(flat_step, 6 * i + a + 1)
                            V.tensor_scalar(half[0], blocks[:, a, :, :, :], 1.0, None, ALU.mult).then_inc(flat_step, 1)
                        else:
                            dve.wait_ge(flat_step, 6 * i + 3 + a)
                            V.tensor_tensor(half[1], blocks[:, a, :, :, :], half[0].bitcast(F32), ALU.subtract
                                            ).then_inc(flat_step, 1)
                for t in range(TILES):
                    evacuate(C_LOOP1 + 1 + 2 * i, 0, v_tok[:, i, t, :], r[t], t)
            for n in range(LEAD, PAIRS + LEAD):
                split(C_KW, n, NC if n < PAIRS else N_GATE)
            evacuate(C_KW, 1, tok_a[:, 1, :], r[1])
            for n in range(LEAD, PAIRS + LEAD):
                split(C_GA, n, NC if n >= PAIRS else N_GATE)
            dve.wait_ge(weights_used, PAIRS * (C_GA + 1))
            for t in range(TILES):
                V.scalar_tensor_tensor(gates[:, t, :, :].rearrange("p h b -> p (h b)"), acc[:, 0, t, 0:N_GATE], r[t],
                                       b_gate, ALU.mult, ALU.add).then_inc(acc0_free if t == 0 else acc1_free, 1)
            for n in range(LEAD, PAIRS + LEAD):
                split(C_CMP, n)
                if n - LEAD == 2:
                    dve.wait_ge(gate_exp, 1)
                    link(V.tensor_scalar(gates[:, :, :, :], gates[:, :, :, :], 1.0, None, ALU.add))
                    link(V.reciprocal(gates[:, :, :, :], gates[:, :, :, :]))
                    for t in range(TILES):
                        link(V.tensor_scalar(gates[:, t, :, 0], gates[:, t, :, 0], any_cmp[:, t:t + 1], None, ALU.mult))
            dve.wait_ge(weights_used, PAIRS * (C_CMP + 1))
            for v in range(2):
                rows, cols = slice(64 * v, 64 * v + 64), slice(CMP_HIDDEN * v, CMP_HIDDEN * (v + 1))
                V.tensor_copy(hidden[rows, :], acc[rows, 1, 0, cols]).then_inc(acc0_free if v == 0 else acc1_free, 1)
            for n in range(LEAD, PAIRS + LEAD):
                split(C_QA0, n)
                if n == LEAD:
                    dve.wait_ge(acc0_free, C_CMP + 1)
                    dve.wait_ge(acc1_free, C_CMP + 1)
                    V.tensor_tensor(gelu[:, :], hidden[:, :], hidden[:, :], ALU.mult).then_inc(gelu_step, 1)
                    dve.wait_ge(gelu_step, 1)
                    V.tensor_scalar(gelu[:, :], gelu[:, :], 0.044715, 1.0, ALU.mult, ALU.add).then_inc(gelu_step, 1)
                    dve.wait_ge(gelu_step, 2)
                    V.tensor_tensor(gelu[:, :], gelu[:, :], hidden[:, :], ALU.mult).then_inc(gelu_step, 1)
                if n == LEAD + 3:
                    dve.wait_ge(tanh_done, 1)
                    V.scalar_tensor_tensor(gelu[:, :], gelu[:, :], 1.0, hidden[:, :], ALU.add, ALU.mult
                                           ).then_inc(gelu_ready, 1)
            evacuate(C_QA0, 0, tok_a[:, 1, :], rq1)

            def mask_unit(u, slot, unit, bias):
                t, h0, nh = UNITS[u]
                nk = P * (t + 1)
                b = (bias[:, 0:P] if t == 0 else bias[:, P:3 * P]).unsqueeze(1).broadcast_to([P, nh, nk])
                p = probs[:, slot, :].rearrange("p (h n) -> p h n", h=nh)
                dve.wait_ge(scores_done, unit + 1)
                V.tensor_tensor(p, scores[:, :].rearrange("p (h n) -> p h n", h=nh), b, ALU.add
                                ).then_inc(scores_free, 1)
                dve.wait_ge(scores_free, unit + 1)
                V.tensor_reduce(negmax[:, slot, 0:nh], p, AX.X, ALU.max, negate=True).then_inc(max_ready, 1)

            def normalise_unit(u, slot, unit, recips, weights=None, gate=None):
                t, h0, nh = UNITS[u]
                nk = P * (t + 1)
                p = probs[:, slot, :].rearrange("p (h n) -> p h n", h=nh)
                f = rden[:, slot, 0:nh]
                dve.wait_ge(exp_done, unit + 1)
                V.reciprocal(f, den[:, slot, 0:nh]).then_inc(recip_done, 1)
                dve.wait_ge(recip_done, recips + 1)
                if gate is not None:
                    V.tensor_tensor(weight[:, slot, 0:nh], f, gate, ALU.mult).then_inc(weight_done, 1)
                    f = weight[:, slot, 0:nh]
                    dve.wait_ge(weight_done, weights + 1)
                V.tensor_tensor(p, p, f.unsqueeze(2).broadcast_to([P, nh, nk]), ALU.mult).then_inc(probs_ready, 1)

            def attention_a_frame(c, g, unit):
                for n in range(LEAD, PAIRS + LEAD):
                    at = n - LEAD
                    if at == 3:
                        view = scores[:, 0:TILES * HPG * CMP_PAD].rearrange("p (t h c) -> p t h c", t=TILES, h=HPG)
                        dve.wait_ge(scores_done, unit + 1)
                        for t in range(TILES):
                            last = V.tensor_tensor(probs_c[:, t, :, :], view[:, t, :, :],
                                                   cmp_bias[:, t, :].unsqueeze(1).broadcast_to([P, HPG, CMP_PAD]),
                                                   ALU.add)
                        last.then_inc(scores_free, 1)
                        dve.wait_ge(scores_free, unit + 1)
                        V.tensor_reduce(cstat[:, 0, :, :], probs_c[:, :, :, :], AX.X, ALU.max, negate=True
                                        ).then_inc(cmp_step, 1)
                        dve.wait_ge(cmp_step, 4 * g + 1)
                        V.tensor_tensor(probs_c[:, :, :, :], probs_c[:, :, :, :],
                                        cstat[:, 0, :, :].unsqueeze(3).broadcast_to([P, TILES, HPG, CMP_PAD]), ALU.add
                                        ).then_inc(max_ready, 1)
                    if 6 <= at <= 11:
                        u = at - 6
                        mask_unit(u % 3, u % 4, unit + 1 + u, causal)
                    split(c, n)
                    if at == 4:
                        dve.wait_ge(exp_done, unit + 1)
                        V.tensor_reduce(cstat[:, 1, :, :], probs_c[:, :, :, :], AX.X, ALU.add).then_inc(cmp_step, 1)
                        dve.wait_ge(cmp_step, 4 * g + 2)
                        V.reciprocal(cstat[:, 2, :, :], cstat[:, 1, :, :]).then_inc(cmp_step, 1)
                        dve.wait_ge(cmp_step, 4 * g + 3)
                        V.tensor_tensor(cstat[:, 3, :, :], cstat[:, 2, :, :], gates[:, :, bass.ds(HPG * g, HPG), 0],
                                        ALU.mult).then_inc(cmp_step, 1)
                        dve.wait_ge(cmp_step, 4 * g + 4)
                        V.tensor_tensor(probs_c[:, :, :, :], probs_c[:, :, :, :],
                                        cstat[:, 3, :, :].unsqueeze(3).broadcast_to([P, TILES, HPG, CMP_PAD]),
                                        ALU.mult).then_inc(probs_ready, 1)
                    if 7 <= at <= 12:
                        u = at - 7
                        t, h0, nh = UNITS[u % 3]
                        normalise_unit(u % 3, u % 4, unit + 1 + u, 6 * g + u, 6 * g + u,
                                       gates[:, t, bass.ds(HPG * g + h0, nh), 1 + u // 3])
                evacuate(c, 1, tok_b[:, 1, :], r[1])

            def mix_tile(at, group):
                if at not in (1, 2, 3, 4, 5, 6):
                    return
                t, step = (at - 1) // 3, (at - 1) % 3
                base = 8 * group + 4 * t
                m = mixed[:, t, :]
                if step == 0:
                    dve.wait_ge(ez_ready, 2 * group + t + 1)
                    V.tensor_scalar(m, m, 1.0, None, ALU.add).then_inc(silu_step, 1)
                    dve.wait_ge(silu_step, base + 1)
                if step < 2:
                    half = m[:, step * 256:(step + 1) * 256]
                    V.reciprocal(half, half).then_inc(silu_step, 1)
                else:
                    dve.wait_ge(silu_step, base + 3)
                    V.tensor_tensor(m, m, tok_b[:, t, :], ALU.mult).then_inc(silu_step, 1)
                    dve.wait_ge(silu_step, base + 4)
                    dve.wait_ge(heads_done, group + 1)
                    V.tensor_tensor(m, m, heads[:, t, :], ALU.mult).then_inc(mix_ready, 1)

            def store_mixed(at, group, fill):
                if at in (6, 9):
                    t = (at - 6) // 3
                    take_fill(fill + t, mix_t[:, bass.ds(HPG * group, HPG), t * P:(t + 1) * P])

            def mixing_frame(c, group, fill):
                for n in range(LEAD, PAIRS + LEAD):
                    store_mixed(n - LEAD, group, fill)
                    split(c, n)
                    mix_tile(n - LEAD, group)
                evacuate(c, 0, tok_a[:, 1, :], rq1)

            with dve.Fori(0, GROUPS - 1) as g:
                attention_a_frame(C_A + 2 * g, g, UNITS_A * g)
                mixing_frame(C_A + 1 + 2 * g, g, FILL_A + FILLS_A + (FILLS_A + FILLS_FINAL) * g)
            attention_a_frame(C_B - 1, GROUPS - 1, UNIT_B - UNITS_A)
            with dve.Fori(0, GROUPS) as g:
                mixing_frame(C_B + 4 * g, GROUPS - 1 + g, FILL_B + FILLS_B * g)
                for j in range(2):
                    for n in range(LEAD, PAIRS + LEAD):
                        split(C_B + 1 + j + 4 * g, n)
                    evacuate(C_B + 1 + j + 4 * g, (j + 1) % 2, tok_a[:, 1, :] if j == 0 else v_tok[:, 0, 1, :], r[1])
                for n in range(LEAD, PAIRS + LEAD):
                    at = n - LEAD
                    if at in (1, 3, 5):
                        u = (at - 1) // 2
                        mask_unit(u, u, UNIT_B + u + UNITS_B * g, dilated)
                    split(C_B + 3 + 4 * g, n)
                    if at in (2, 4, 6):
                        u = (at - 2) // 2
                        normalise_unit(u, u, UNIT_B + u + UNITS_B * g, 6 * GROUPS + u + UNITS_B * g)
                evacuate(C_B + 3 + 4 * g, 1, tok_b[:, 1, :], r[1])

            def scale_chunk(n, parity, cols, uses):
                dve.wait_ge(weights_used, PAIRS * (C_OUT + n + 1))
                dve.wait_ge(wpost_landed[parity], 16 * uses)
                V.tensor_tensor(y[:, 1, cols], acc[:, parity, 1, :], wpost[:, parity, :], ALU.mult).then_inc(y_scaled, 1)
                dve.wait_ge(y_square, n + 1)
                V.tensor_tensor(y[:, 0, cols], acc[:, parity, 0, :], wpost[:, parity, :], ALU.mult).then_inc(acc0_free, 1)
                dve.wait_ge(acc1_free, C_OUT + n + 1)

            def mix_rest(n):
                dve.wait_ge(mixhi_ready, n + 1)
                V.tensor_tensor(x_lo[:, 2 * n:2 * n + 2, :], mix_t[:, 2 * n:2 * n + 2, :],
                                x_hi[:, 2 * n:2 * n + 2, :].bitcast(F32), ALU.subtract).then_inc(mix_ready_pairs, 1)

            for n in range(LEAD):
                mix_rest(n)
            for n in range(LEAD, PAIRS + LEAD):
                store_mixed(n - LEAD, 2 * GROUPS - 1, FILL_LAST)
                if n < PAIRS:
                    mix_rest(n)
                split(C_OUT, n)
                mix_tile(n - LEAD, 2 * GROUPS - 1)
            scale_chunk(0, 0, slice(0, NC), 1)
            V.tensor_copy(ssum[:, :], ssq[:, 0, :]).then_inc(ssum_done, 1)
            with dve.Fori(0, (N_OUT - 2) // 2) as i:
                for j in range(2):
                    for n in range(LEAD, PAIRS + LEAD):
                        split(C_OUT + 1 + j + 2 * i, n)
                    scale_chunk(1 + j + 2 * i, (j + 1) % 2, bass.ds(NC * (1 + j) + 2 * NC * i, NC),
                                1 + j + i)
                    dve.wait_ge(ssum_done, 1 + j + 2 * i)
                    V.tensor_tensor(ssum[:, :], ssum[:, :], ssq[:, (j + 1) % 2, :], ALU.add).then_inc(ssum_done, 1)
            for n in range(LEAD, PAIRS):
                split(C_OUT + N_OUT - 1, n)
            scale_chunk(N_OUT - 1, 1, slice(NC * (N_OUT - 1), NC * N_OUT), N_OUT // 2)
            dve.wait_ge(ssum_done, N_OUT - 1)
            link(V.tensor_tensor(stat[:, 0, :], ssum[:, :], ssq[:, 1, :], ALU.add))
            variance()
            inverse_rms(2)
            for t in range(TILES):
                dve.wait_ge(xres_landed[t], 16)
                for j in range(4):
                    cols = slice(j * 1024, (j + 1) * 1024)
                    V.scalar_tensor_tensor(y[:, t, cols], y[:, t, cols], r[t], x_tok[:, t, cols], ALU.mult, ALU.add
                                           ).then_inc(y_added, 1)


def constants():
    i, j = np.arange(SEQ)[:, None], np.arange(SEQ)[None, :]
    dist = i - j
    causal = np.where(dist >= 0, 0.0, NEG)
    seen = sum(((dist >= 0) & (dist % d == 0) & (dist // d <= w // d)).astype(int)
               for w, d in ((128, 1), (512, 4), (2048, 16)))
    dilated = np.where(seen > 0, np.log(np.maximum(seen, 1)), NEG)
    c = np.arange(CMP_PAD)[None, :]
    valid = (c * CMP_STRIDE + CMP_LEN - 1 <= i) & (c < N_CMP)
    cmp_bias = np.where(valid, 0.0, NEG)
    tok = lambda a: a.reshape(TILES, P, -1).transpose(1, 0, 2).reshape(P, -1)
    two = lambda a: np.concatenate([a[:P, :P], a[P:, :]], axis=1)
    half = HEAD // 2
    inv = np.float32(ROPE_THETA) ** (-np.arange(half, dtype=np.float32) / np.float32(half))
    return [np.eye(P), two(causal), two(dilated), tok(cmp_bias), tok(valid.any(axis=1, keepdims=True)),
            np.broadcast_to(inv, (P, half))]


def kernel(x, positions, pre_norm_w, post_norm_w, w_in, b_gate, cmp_pe_k, cmp_pe_v,
           cmp_wk1, cmp_wk2, cmp_wv1, cmp_wv2, w_out):
    import concourse.bacc as bacc
    from concourse.bass_utils import run_bass_kernel_spmd

    f = lambda a: np.asarray(a, dtype=np.float32)
    x = np.ascontiguousarray(f(x)[0])
    pe = np.stack([f(cmp_pe_k)[0].T, f(cmp_pe_v)[0].T], axis=1).reshape(P, 2 * CMP_LEN)
    table = np.concatenate([a.astype(np.float32) for a in constants()] + [
        pe, np.broadcast_to(f(b_gate)[0], (P, N_GATE))], axis=1)
    arrays = {
        "in_x": x,
        "in_x_t": np.ascontiguousarray(x.T),
        "in_positions": np.ascontiguousarray(np.asarray(positions, dtype=np.int32)[0].reshape(TILES, P).T),
        "in_norm": np.ascontiguousarray(f(pre_norm_w)[0].reshape(KB, P).T),
        "in_table": np.ascontiguousarray(table),
        "in_w_in": np.ascontiguousarray(f(w_in)[0]),
        "in_w1": np.concatenate([f(cmp_wk1)[0], f(cmp_wv1)[0]], axis=1),
        "in_w2": np.ascontiguousarray(np.stack([f(cmp_wk2)[0], f(cmp_wv2)[0]]).reshape(2, 2, P, P).transpose(2, 0, 1, 3)),
        "in_post_w": np.ascontiguousarray(f(post_norm_w)),
        "in_w_out": np.ascontiguousarray(f(w_out)[0]),
    }
    nc = bacc.Bacc("TRN2", target_bir_lowering=False, num_devices=1, dynamic_dma_scratch_size=1024)
    t = {n: nc.dram_tensor(n, a.shape, mybir.dt.from_np(a.dtype), kind="ExternalInput").ap()
         for n, a in arrays.items()}
    out = nc.dram_tensor("out_0", (SEQ, D_MODEL), F32, kind="ExternalOutput").ap()
    build(nc, t["in_x"], t["in_x_t"], t["in_positions"], t["in_norm"], t["in_table"], t["in_w_in"], t["in_w1"], t["in_w2"],
          t["in_post_w"], t["in_w_out"], out)
    r = run_bass_kernel_spmd(nc, [arrays], core_ids=[0])
    return r.results[0]["out_0"].reshape(1, SEQ, D_MODEL)
```

```python
import math
from contextlib import ExitStack

import concourse.bass as bass
import numpy as np
from concourse import mybir
from concourse.alu_op_type import AluOpType as ALU

F32 = mybir.dt.float32
F32R = mybir.dt.float32r
I32 = mybir.dt.int32
ACT = mybir.ActivationFunctionType
AX = mybir.AxisListType

P = 128
D_MODEL, SEQ, HEAD = 4096, 256, 128
TILES = SEQ // P
KB = D_MODEL // P
PAIRS = KB // 2
NC = 512
GROUPS = 4
HPG = 4
N_HEADS = 16
N_GATE = 3 * N_HEADS
CMP_LEN, CMP_STRIDE, CMP_HIDDEN = 32, 16, 256
N_CMP = SEQ // CMP_STRIDE - 1
CMP_PAD = 16
SCALE = HEAD ** -0.5
EPS = 1e-6
NEG = -1e30
ROPE_THETA = 10000.0
RAW_SLOTS, SPLIT_SLOTS, LEAD = 4, 4, 3
WARM_UP = 12

_SIZES = [2048, 2048, N_GATE] + [512] * 6 + [2048] * 4
QA, ZA, GA, KC, VC, KSL, VSL, KW, VW, QB, KBC, VB, ZB = [sum(_SIZES[:i]) for i in range(13)]

C_KSL = 0
C_LOOP1 = 1
C_KW, C_CMP, C_QA0 = 5, 6, 7
C_A = 8
C_B = C_A + 2 * GROUPS - 1
C_OUT = C_B + 4 * GROUPS
N_OUT = D_MODEL // NC

FILL_KSL, FILL_GATE, FILL_KW, FILL_CMP, FILL_A = 4, 6, 7, 9, 12
FILLS_A, FILLS_FINAL = 12, 2
FILL_B = FILL_A + GROUPS * (FILLS_A + FILLS_FINAL) - FILLS_FINAL
FILLS_B = FILLS_FINAL + 2 + 2 + 3
FILL_LAST = FILL_B + GROUPS * FILLS_B
UNITS_A, UNITS_B = 7, 3
UNIT_B = GROUPS * UNITS_A
UNITS = [(0, 0, 4), (1, 0, 2), (1, 2, 2)]
XT_PIECES = [(0, 2), (2, 4)] + [(k, k + 4) for k in range(4, KB, 4)]
OUT_COLS = 512
OUT_PIECES = [(t, c) for t in range(TILES) for c in range(0, D_MODEL, OUT_COLS)]
POOL_PIECES = [3, 6, 11, 14]
OUT_TRANSFERS = [(0, 1), (1, 2)] + [(i, i + 2) for i in range(2, len(OUT_PIECES), 2)]
CONST_COLS = 128 + 384 + 384 + 2 * CMP_PAD + TILES + 64 + 2 * CMP_LEN + N_GATE + 1


def build(nc, x, x_t, positions, norm_cols, consts, w_in, w1, w2, post_w, w_out, out):
    ctx = ExitStack()
    with ctx:
        at = [1152]

        def sb(name, shape, dt=F32, offset=None):
            size = 4 * math.prod(shape[1:])
            where = at[0] if offset is None else offset
            if offset is None:
                at[0] += (size + 31) // 32 * 32
            t = nc.alloc_sbuf_tensor_at(name, shape, dt, offset=where)
            return t, where

        x_parts, _ = sb("x_parts", [P, KB, 2, SEQ], F32R)
        x_hi, x_lo = x_parts[:, :, 0, :], x_parts[:, :, 1, :]
        mix_t, region = sb("mix_t", [P, KB, SEQ])
        xt_raw, _ = sb("xt_raw", [P, KB, SEQ], offset=region)
        flat_hi, _ = sb("flat_hi", [P, CMP_LEN, P], F32R, offset=region)
        flat_lo, _ = sb("flat_lo", [P, CMP_LEN, P], F32R, offset=region + 4 * CMP_LEN * P)
        y, _ = sb("y", [P, TILES, D_MODEL], offset=region)
        raw, _ = sb("raw", [P, RAW_SLOTS, 2, NC])
        w_hi, _ = sb("w_hi", [P, SPLIT_SLOTS, 2, NC], F32R)
        w_lo, _ = sb("w_lo", [P, SPLIT_SLOTS, 2, NC], F32R)
        k_t, late = sb("k_t", [P, 2, HPG, SEQ])
        v_tok, _ = sb("v_tok", [P, 2, TILES, NC])
        qraw_t, q_off = sb("qraw_t", [P, HPG, SEQ])
        qrot_t, _ = sb("qrot_t", [P, HPG, SEQ])
        probs, p_off = sb("probs", [P, 4, NC])
        x_tok, _ = sb("x_tok", [P, TILES, D_MODEL], offset=late)
        blocks, _ = sb("blocks", [P, 2, HPG, N_CMP, CMP_STRIDE], offset=p_off)
        gate_raw, _ = sb("gate_raw", [P, KB, N_GATE], offset=q_off)
        probs_t, pt_off = sb("probs_t", [P, 2, NC])
        mixed, _ = sb("mixed", [P, TILES, NC])
        wpost, _ = sb("wpost", [P, 2, NC])
        gate_w, _ = sb("gate_w", [P, KB, 2 * N_GATE], F32R, offset=pt_off)
        tok_a, _ = sb("tok_a", [P, TILES, NC])
        tok_b, _ = sb("tok_b", [P, TILES, NC])
        rot, _ = sb("rot", [P, TILES, NC])
        rot_tmp, _ = sb("rot_tmp", [P, NC])
        cst, _ = sb("cst", [P, CONST_COLS])
        pos_i, _ = sb("pos_i", [P, TILES], I32)
        pos_f, _ = sb("pos_f", [P, TILES])
        trig, _ = sb("trig", [P, 2, TILES, 64])
        turns, _ = sb("turns", [P, 2, TILES, 64])
        w2_sb, _ = sb("w2_sb", [P, 2, 2, P])
        hidden, _ = sb("hidden", [P, CMP_HIDDEN])
        gelu, _ = sb("gelu", [P, CMP_HIDDEN])
        hid_t, _ = sb("hid_t", [P, 2, P])
        kc_t, _ = sb("kc_t", [P, GROUPS * CMP_PAD])
        vc, _ = sb("vc", [CMP_PAD, GROUPS, HEAD])
        gates, _ = sb("gates", [P, TILES, N_HEADS, 3])
        probs_c, _ = sb("probs_c", [P, TILES, HPG, CMP_PAD])
        negmax, _ = sb("negmax", [P, 4, HPG])
        den, _ = sb("den", [P, 4, HPG])
        rden, _ = sb("rden", [P, 4, HPG])
        weight, _ = sb("weight", [P, 4, HPG])
        cstat, _ = sb("cstat", [P, 4, TILES, HPG])
        stat, _ = sb("stat", [P, 8, TILES])
        scl, _ = sb("scl", [P, 2, TILES])
        ssq, _ = sb("ssq", [P, 2, TILES])
        ssum, _ = sb("ssum", [P, TILES])
        junk, _ = sb("junk", [P, NC])
        gate_sum = junk[0:2 * N_GATE, 0:SEQ]
        assert at[0] <= nc.sbuf_usable_end, at[0]

        norm_w, _ = sb("norm_w", [P, KB])
        assert at[0] <= nc.sbuf_usable_end, at[0]
        col = 0

        def const(width):
            nonlocal col
            col += width
            return cst[:, col - width:col]

        ident = const(P)
        causal, dilated = const(384), const(384)
        cmp_bias = const(TILES * CMP_PAD).rearrange("p (t c) -> p t c", t=TILES)
        any_cmp = const(TILES)
        inv_freq = const(64)
        pe_t = const(2 * CMP_LEN).rearrange("p (v a b) -> p v a b", v=2, a=2)
        b_gate = const(N_GATE)
        ones = const(1)

        def psum(name, shape):
            return ctx.enter_context(nc.psum_tensor(name, shape, F32))

        acc = psum("acc", [P, 2, TILES, NC])
        scores = psum("scores", [P, NC])
        trans = psum("trans", [P, NC])
        heads = psum("heads", [P, TILES, NC])

        def sem(name):
            return ctx.enter_context(nc.semaphore(name))

        raw_landed = [sem(f"raw_landed{i}") for i in range(RAW_SLOTS)]
        norm_landed = sem("norm_landed")
        zeros_ready = sem("zeros_ready")
        consts_landed = sem("consts_landed")
        w2_landed = sem("w2_landed")
        xt_landed = [sem(f"xt_landed{i}") for i in range(len(XT_PIECES))]
        gate_landed = sem("gate_landed")
        xres_landed = sem("xres_landed")
        wpost_landed = [sem(f"wpost_landed{i}") for i in range(2)]
        hi_ready = sem("hi_ready")
        lo_ready = sem("lo_ready")
        weights_used = sem("weights_used")
        xhi_ready = sem("xhi_ready")
        x_ready = sem("x_ready")
        mixhi_ready = sem("mixhi_ready")
        mix_ready_pairs = sem("mix_ready_pairs")
        acc0_free = sem("acc0_free")
        acc1_free = sem("acc1_free")
        tr_done = sem("tr_done")
        tr_free = sem("tr_free")
        scores_done = sem("scores_done")
        scores_free = sem("scores_free")
        max_ready = sem("max_ready")
        exp_done = sem("exp_done")
        recip_done = sem("recip_done")
        weight_done = sem("weight_done")
        probs_ready = sem("probs_ready")
        heads_done = sem("heads_done")
        rope_muls = sem("rope_muls")
        rope_subs = sem("rope_subs")
        rope_done = sem("rope_done")
        ez_ready = sem("ez_ready")
        silu_step = sem("silu_step")
        mix_ready = sem("mix_ready")
        chain = sem("chain")
        angles_ready = sem("angles_ready")
        trig_ready = sem("trig_ready")
        squares_done = sem("squares_done")
        squares_added = sem("squares_added")
        sumsq_done = sem("sumsq_done")
        gatew_step = sem("gatew_step")
        gate_done = sem("gate_done")
        gate_moved = sem("gate_moved")
        var_ready = sem("var_ready")
        rms_ready = sem("rms_ready")
        stats_ready = sem("stats_ready")
        root_done = sem("root_done")
        flat_zeroed = sem("flat_zeroed")
        flat_step = sem("flat_step")
        gate_exp = sem("gate_exp")
        cmp_step = sem("cmp_step")
        gelu_step = sem("gelu_step")
        gelu_ready = sem("gelu_ready")
        tanh_done = sem("tanh_done")
        y_square = sem("y_square")
        y_scaled = sem("y_scaled")
        ssum_done = sem("ssum_done")
        y_rescaled = sem("y_rescaled")
        y_added = sem("y_added")
        y_added_pool = sem("y_added_pool")
        final_ready = sem("final_ready")
        last_tile0 = sem("last_tile0")
        out_done = sem("out_done")

        block = ctx.enter_context(nc.Block())

        w_in_v = w_in.rearrange("(k p) c -> p k c", p=P)
        w1_v = w1.rearrange("(k p) c -> p k c", p=P)
        w_out_v = w_out.rearrange("(k p) c -> p k c", p=P)
        x_v = x.rearrange("(t p) d -> p t d", p=P)
        xt_v = x_t.rearrange("(k p) t -> p k t", p=P)
        out_v = out.rearrange("(t p) d -> p t d", p=P)

        def lag(v):
            return not isinstance(v, int) or v > 0

        @block.sync
        def _(sp):
            def load_pair(src, c, n, col, width=NC):
                first = sp.snap(col) if not isinstance(col, int) else col
                if lag(16 * c + n - RAW_SLOTS + 1):
                    sp.wait_ge(lo_ready, 16 * c + (n - RAW_SLOTS + 1))
                sp.dma_start(raw[:, n % RAW_SLOTS, :, 0:width],
                             src[:, 2 * n:2 * n + 2, bass.ds(first, width)]
                             ).then_inc(raw_landed[n % RAW_SLOTS], 16)

            def load_chunk(src, c, col, width=NC, start=0):
                for n in range(start, PAIRS):
                    load_pair(src, c, n, col, width)

            for n in range(PAIRS):
                for j, (a, b) in enumerate(XT_PIECES):
                    if j > 0 and 2 * n < a <= 2 * n + 2:
                        sp.dma_start(xt_raw[:, a:b, :], xt_v[:, a:b, :]).then_inc(xt_landed[j], 16)
                load_pair(w_in_v, C_KSL, n, KSL)
                if n == 6:
                    sp.dma_start(cst[:, :], consts).then_inc(consts_landed, 16)
                    sp.dma_start(pos_i[:, :], positions).then_inc(consts_landed, 16)
            sp.dma_start(gate_raw[:, :, :], w_in_v[:, :, GA:GA + N_GATE]).then_inc(gate_landed, 16)
            sp.dma_start(w2_sb[:, :, :, :], w2).then_inc(w2_landed, 16)
            with sp.Fori(0, 2) as i:
                load_chunk(w_in_v, C_LOOP1 + 2 * i, KC + (VC - KC) * i)
                load_chunk(w_in_v, C_LOOP1 + 1 + 2 * i, VSL + (VW - VSL) * i)
            load_chunk(w_in_v, C_KW, KW)
            load_chunk(w1_v, C_CMP, 0)
            load_chunk(w_in_v, C_QA0, QA)
            with sp.Fori(0, GROUPS - 1) as g:
                load_chunk(w_in_v, C_A + 2 * g, ZA + NC * g)
                load_chunk(w_in_v, C_A + 1 + 2 * g, QA + NC + NC * g)
            load_chunk(w_in_v, C_B - 1, ZA + NC * (GROUPS - 1))
            with sp.Fori(0, GROUPS) as g:
                load_chunk(w_in_v, C_B + 4 * g, QB + NC * g)
                load_chunk(w_in_v, C_B + 1 + 4 * g, KBC + NC * g)
                load_chunk(w_in_v, C_B + 2 + 4 * g, VB + NC * g)
                load_chunk(w_in_v, C_B + 3 + 4 * g, ZB + NC * g)
            for j in range(2):
                sp.dma_start(wpost[:, j, :], post_w[0:1, j * NC:(j + 1) * NC].broadcast_to([P, NC])
                             ).then_inc(wpost_landed[j], 16)
            load_chunk(w_out_v, C_OUT, 0)
            sp.wait_ge(weights_used, PAIRS * C_OUT)

            def load_residual(col):
                first = sp.snap(col) if not isinstance(col, int) else col
                for t in range(TILES):
                    sp.dma_start(x_tok[:, t, bass.ds(first, NC)], x_v[:, t, bass.ds(first, NC)]
                                 ).then_inc(xres_landed, 16)

            def load_post(j, c, col):
                first = sp.snap(col)
                sp.wait_ge(acc0_free, c - 1)
                sp.wait_ge(acc1_free, c - 1)
                sp.dma_start(wpost[:, j, :], post_w[0:1, bass.ds(first, NC)].broadcast_to([P, NC])
                             ).then_inc(wpost_landed[j], 16)

            load_chunk(w_out_v, C_OUT + 1, NC)
            for j in range(2):
                load_residual(j * NC)
            with sp.Fori(0, (N_OUT - 2) // 2) as i:
                for j in range(2):
                    load_chunk(w_out_v, C_OUT + 2 + j + 2 * i, NC * (2 + j) + 2 * NC * i)
                    load_post(j, C_OUT + 2 + j + 2 * i, NC * (2 + j) + 2 * NC * i)
                    load_residual(NC * (2 + j) + 2 * NC * i)
            for first, after in OUT_TRANSFERS:
                for i in range(first, after):
                    if i in POOL_PIECES:
                        sp.wait_ge(y_added_pool, POOL_PIECES.index(i) + 1)
                    else:
                        sp.wait_ge(y_added, i + 1 - sum(p < i for p in POOL_PIECES))
                t, c = OUT_PIECES[first]
                cols = slice(c, c + (after - first) * OUT_COLS)
                sp.dma_start(out_v[:, t, cols], y[:, t, cols]).then_inc(out_done, 16)
            sp.wait_ge(out_done, 16 * len(OUT_TRANSFERS))

        @block.gpsimd
        def _(pool):
            total = rot[:, 0, :].rearrange("p (k t) -> p k t", k=2)
            square = rot_tmp[:, :].rearrange("p (k t) -> p k t", k=2)
            for n in range(PAIRS):
                pair = xt_raw[:, 2 * n:2 * n + 2, :]
                piece = [i for i, (a, b) in enumerate(XT_PIECES) if a <= 2 * n < b][0]
                pool.wait_ge(xt_landed[piece], 16)
                if n == 0:
                    nc.gpsimd.tensor_tensor(total, pair, pair, ALU.mult).then_inc(squares_added, 1)
                else:
                    nc.gpsimd.tensor_tensor(square, pair, pair, ALU.mult).then_inc(squares_done, 1)
                    pool.wait_ge(squares_done, n)
                    pool.wait_ge(squares_added, n)
                    nc.gpsimd.tensor_tensor(total, total, square, ALU.add).then_inc(squares_added, 1)
                    pool.wait_ge(squares_added, n + 1)
            pool.wait_ge(sumsq_done, 1)
            pool.wait_ge(x_ready, PAIRS)
            for half in (flat_hi, flat_lo):
                pad = half[:, :, :].rearrange("p l (v c) -> p l v c", c=CMP_PAD)[:, :, :, CMP_PAD - 1:CMP_PAD]
                nc.gpsimd.memset(pad.bitcast(F32), 0.0).then_inc(flat_zeroed, 1)

            def rope(src, t, chunk, tile_no):
                pool.wait_ge(acc0_free if t == 0 else acc1_free, chunk + 1)
                s4 = src[:, t, :].rearrange("p (h x d) -> p h x d", h=HPG, x=2)
                r4 = rot[:, t, :].rearrange("p (h x d) -> p h x d", h=HPG, x=2)
                m4 = rot_tmp[:, :].rearrange("p (h x d) -> p h x d", h=HPG, x=2)
                sin = trig[:, 0, t, :].unsqueeze(1).broadcast_to([P, HPG, 64])
                cos = trig[:, 1, t, :].unsqueeze(1).unsqueeze(1).broadcast_to([P, HPG, 2, 64])
                nc.gpsimd.tensor_tensor(r4, s4, cos, ALU.mult).then_inc(rope_muls, 1)
                nc.gpsimd.tensor_tensor(m4[:, :, 0, :], s4[:, :, 1, :], sin, ALU.mult).then_inc(rope_muls, 1)
                nc.gpsimd.tensor_tensor(m4[:, :, 1, :], s4[:, :, 0, :], sin, ALU.mult).then_inc(rope_muls, 1)
                pool.wait_ge(rope_muls, 3 * tile_no + 3)
                nc.gpsimd.tensor_tensor(r4[:, :, 0, :], r4[:, :, 0, :], m4[:, :, 0, :], ALU.subtract
                                        ).then_inc(rope_subs, 1)
                nc.gpsimd.tensor_tensor(r4[:, :, 1, :], r4[:, :, 1, :], m4[:, :, 1, :], ALU.add
                                        ).then_inc(rope_done, 1)
                pool.wait_ge(rope_subs, tile_no + 1)
                pool.wait_ge(rope_done, tile_no + 1)

            pool.wait_ge(trig_ready, 1)
            for t in range(TILES):
                rope(tok_b, t, C_KSL, t)
            for t in range(TILES):
                rope(tok_a, t, C_KW, 2 + t)
            for t in range(TILES):
                rope(tok_a, t, C_QA0, 4 + t)
            with pool.Fori(0, GROUPS - 1) as g:
                for t in range(TILES):
                    rope(tok_a, t, C_A + 1 + 2 * g, 6 + t + 2 * g)
            with pool.Fori(0, GROUPS) as g:
                for j in range(2):
                    for t in range(TILES):
                        rope(tok_a, t, C_B + j + 4 * g, 12 + 2 * j + t + 4 * g)

            for i, piece in enumerate(POOL_PIECES):
                t, c = OUT_PIECES[piece]
                if i == 0:
                    pool.wait_ge(xres_landed, 16 * TILES * N_OUT)
                pool.wait_ge(y_rescaled, i + 1)
                nc.gpsimd.tensor_tensor(y[:, t, c:c + OUT_COLS], y[:, t, c:c + OUT_COLS],
                                        x_tok[:, t, c:c + OUT_COLS], ALU.add).then_inc(y_added_pool, 1)

        @block.tensor
        def _(pe):
            def gemm_pair(c, n, parity, width=NC, hi=x_hi, lo=x_lo, tiles=range(TILES), ready=None, wait_banks=True):
                if n == 0 and wait_banks:
                    pe.wait_ge(acc0_free, c - 1)
                    pe.wait_ge(acc1_free, c - 1)
                if ready is not None:
                    pe.wait_ge(ready, n + 1)
                pe.wait_ge(lo_ready, 16 * c + n + 1)
                s = n % SPLIT_SLOTS
                for kk in range(2):
                    k = 2 * n + kk
                    for t in tiles:
                        o = acc[:, parity, t, 0:width]
                        stat_hi, stat_lo = hi[:, k, t * P:(t + 1) * P], lo[:, k, t * P:(t + 1) * P]
                        nc.tensor.matmul(o, stat_hi, w_hi[:, s, kk, 0:width], start=(k == 0), stop=False)
                        nc.tensor.matmul(o, stat_hi, w_lo[:, s, kk, 0:width], start=False, stop=False)
                        last = nc.tensor.matmul(o, stat_lo, w_hi[:, s, kk, 0:width],
                                                start=False, stop=(k == KB - 1))
                if tiles != (0,):
                    last.then_inc(weights_used, 1)
                elif n == PAIRS - 1:
                    last.then_inc(last_tile0, 1)

            def transpose4(src, fill):
                if fill is not None:
                    pe.wait_ge(tr_free, fill)
                for b in range(4):
                    last = nc.tensor.transpose(trans[:, b * P:(b + 1) * P], src[:, b * P:(b + 1) * P], ident)
                last.then_inc(tr_done, 1)

            def rotated(t, tile_no, fill):
                pe.wait_ge(rope_done, tile_no + 1)
                transpose4(rot[:, t, :], fill)

            def unit_scores(u, unit, q_t, keys, fills):
                t, h0, nh = UNITS[u]
                pe.wait_ge(tr_free, fills)
                pe.wait_ge(scores_free, unit)
                nk = P * (t + 1)
                for i in range(nh):
                    last = nc.tensor.matmul(scores[:, i * nk:(i + 1) * nk], q_t[:, h0 + i, t * P:(t + 1) * P],
                                            keys(h0 + i, nk), start=True, stop=True)
                last.then_inc(scores_done, 1)

            def unit_transpose(slot, unit, fill):
                pe.wait_ge(probs_ready, unit + 1)
                transpose4(probs[:, slot, :], fill)

            def unit_values(u, slot, values, fill, first, last_one):
                t, h0, nh = UNITS[u]
                pe.wait_ge(tr_free, fill + 1)
                for i in range(nh):
                    for b in range(t + 1):
                        blk = i * (t + 1) + b
                        last = nc.tensor.matmul(heads[:, t, (h0 + i) * P:(h0 + i + 1) * P],
                                                probs_t[:, slot % 2, blk * P:(blk + 1) * P], values(h0 + i, b),
                                                start=(first and blk == 0), stop=(last_one and b == t),
                                                skip_group_check=True)
                return last

            def attention_a(n, c, g, fill, unit, tiles_rotated):
                if n in (1, 2):
                    t = n - 1
                    pe.wait_ge(acc0_free if t == 0 else acc1_free, c)
                    transpose4(tok_a[:, t, :], fill + t)
                if n == 3:
                    pe.wait_ge(tr_free, fill + 2)
                    for t in range(TILES):
                        for h in range(HPG):
                            o = (t * HPG + h) * CMP_PAD
                            last = nc.tensor.matmul(scores[:, o:o + CMP_PAD], qraw_t[:, h, t * P:(t + 1) * P],
                                                    kc_t[:, bass.ds(CMP_PAD * g, CMP_PAD)], start=True, stop=True)
                    last.then_inc(scores_done, 1)
                if n in (4, 5):
                    rotated(n - 4, tiles_rotated + n - 4, fill + n - 2)
                if n in (6, 7):
                    t = n - 6
                    pe.wait_ge(probs_ready, unit + 1)
                    pe.wait_ge(tr_free, fill + 4 + t)
                    for h in range(HPG):
                        last = nc.tensor.transpose(trans[0:CMP_PAD, h * P:(h + 1) * P], probs_c[:, t, h, :], ident)
                    last.then_inc(tr_done, 1)
                if n in (8, 9):
                    pe.wait_ge(tr_free, fill + n - 3)
                if 6 <= n <= 11:
                    u = n - 6
                    keys = lambda h, nk: k_t[:, u // 3, g, 0:nk]
                    unit_scores(u % 3, unit + 1 + u, qrot_t, keys, fill + 4)
                if n in (8, 9):
                    t = n - 8
                    for h in range(HPG):
                        nc.tensor.matmul(heads[:, t, h * P:(h + 1) * P], probs_t[0:CMP_PAD, t, h * P:(h + 1) * P],
                                         vc[0:CMP_PAD, g, :],
                                         start=(h == 0), stop=False, skip_group_check=True)
                if 10 <= n:
                    u = n - 10
                    values = lambda h, b: v_tok[:, u // 3, b, bass.ds(P * g, P)]
                    last = unit_values(u % 3, u, values, fill + 6 + u, False, u >= 3)
                    if n == PAIRS - 1:
                        last.then_inc(heads_done, 1)
                if 9 <= n <= 14:
                    u = n - 9
                    unit_transpose(u % 4, unit + 1 + u, fill + 6 + u)

            def attention_b(n, fill, unit):
                if n in (1, 3, 5):
                    u = (n - 1) // 2
                    unit_scores(u, unit + u, qrot_t, lambda h, nk: k_t[:, 0, h, 0:nk], fill)
                if n in (4, 6, 8):
                    u = (n - 4) // 2
                    unit_transpose(u, unit + u, fill + u)
                if n in (5, 7, 9):
                    u = (n - 5) // 2
                    last = unit_values(u, u, lambda h, b: v_tok[:, 0, b, h * P:(h + 1) * P], fill + u,
                                       u < 2, True)
                    if u == 2:
                        last.then_inc(heads_done, 1)

            def final(n, fill, tiles_mixed):
                if n in (6, 10):
                    t = (n - 6) // 4
                    pe.wait_ge(mix_ready, tiles_mixed + t + 1)
                    transpose4(mixed[:, t, :], fill + t)

            pe.wait_ge(zeros_ready, 2)
            for i in range(WARM_UP):
                nc.tensor.matmul(scores[:, 0:CMP_HIDDEN], hidden[:, 0:P], hidden[:, :], start=True, stop=True)
            for n in range(PAIRS):
                gemm_pair(C_KSL, n, 1, ready=x_ready, wait_banks=False)
            pe.wait_ge(consts_landed, 16 * 2)
            pe.wait_ge(squares_added, PAIRS)
            for t in range(TILES):
                for k in range(2):
                    last = nc.tensor.matmul(trans[:, t:t + 1], rot[:, 0, k * SEQ + t * P:k * SEQ + (t + 1) * P], ones,
                                            start=(k == 0), stop=(k == 1))
            last.then_inc(sumsq_done, 1)
            with pe.Fori(0, 2) as i:
                for n in range(PAIRS):
                    gemm_pair(C_LOOP1 + 2 * i, n, 0, wait_banks=False)
                for n in range(PAIRS):
                    if n in (1, 2):
                        pe.wait_ge(acc0_free if n == 1 else acc1_free, 2 * i + 2)
                        transpose4(tok_a[:, n - 1, :], None if n == 1 else 2 * i + 1)
                    gemm_pair(C_LOOP1 + 1 + 2 * i, n, 1)
            for n in range(PAIRS):
                if n in (4, 5):
                    rotated(n - 4, n - 4, FILL_KSL + n - 4)
                if n == 6:
                    pe.wait_ge(gatew_step, 2)
                    for k in range(KB):
                        last = nc.tensor.matmul(scores[0:2 * N_GATE, :], gate_w[:, k, :], x_parts[:, k, :, :],
                                                start=(k == 0), stop=(k == KB - 1))
                    last.then_inc(gate_done, 1)
                gemm_pair(C_KW, n, 0)
            pe.wait_ge(flat_step, 2 * 6)
            for n in range(PAIRS):
                if n == 2:
                    pe.wait_ge(gate_moved, 2)
                    pe.wait_ge(tr_free, FILL_GATE)
                    for t in range(TILES):
                        for j in range(2):
                            last = nc.tensor.matmul(trans[:, t * N_GATE:(t + 1) * N_GATE],
                                                    gate_sum[:, t * P:(t + 1) * P],
                                                    ident[0:2 * N_GATE, j * N_GATE:(j + 1) * N_GATE],
                                                    start=(j == 0), stop=(j == 1))
                    last.then_inc(tr_done, 1)
                if n in (7, 8):
                    rotated(n - 7, 2 + n - 7, FILL_KW + n - 7)
                gemm_pair(C_CMP, n, 1, hi=flat_hi, lo=flat_lo, tiles=range(1))
            for n in range(PAIRS):
                if n == 5:
                    pe.wait_ge(gelu_ready, 1)
                    pe.wait_ge(w2_landed, 16)
                    pe.wait_ge(tr_free, FILL_CMP)
                    for j in range(2):
                        last = nc.tensor.transpose(trans[:, j * P:(j + 1) * P], gelu[:, j * P:(j + 1) * P], ident)
                    last.then_inc(tr_done, 1)
                if n == 6:
                    pe.wait_ge(tr_free, FILL_CMP + 1)
                    for j in range(2):
                        last = nc.tensor.matmul(trans[:, 0:64], w2_sb[:, 0, j, :], hid_t[:, j, 0:64],
                                                start=(j == 0), stop=(j == 1))
                    last.then_inc(tr_done, 1)
                if n == 7:
                    pe.wait_ge(tr_free, FILL_CMP + 2)
                    for h in range(GROUPS):
                        for j in range(2):
                            c0 = 64 + h * CMP_PAD
                            last = nc.tensor.matmul(trans[0:CMP_PAD, h * P:(h + 1) * P], hid_t[:, j, c0:c0 + CMP_PAD],
                                                    w2_sb[:, 1, j, :], start=(j == 0), stop=(j == 1))
                    last.then_inc(tr_done, 1)
                gemm_pair(C_QA0, n, 0)

            def attention_a_chunk(c, g, fill, unit, tiles_rotated):
                for n in range(PAIRS):
                    attention_a(n, c, g, fill, unit, tiles_rotated)
                    gemm_pair(c, n, 1)

            with pe.Fori(0, GROUPS - 1) as g:
                per = FILLS_A + FILLS_FINAL
                attention_a_chunk(C_A + 2 * g, g, FILL_A + per * g, UNITS_A * g, 4 + 2 * g)
                for n in range(PAIRS):
                    final(n, FILL_A + FILLS_A + per * g, 2 * g)
                    gemm_pair(C_A + 1 + 2 * g, n, 0)
            attention_a_chunk(C_B - 1, GROUPS - 1, FILL_B - FILLS_A, UNIT_B - UNITS_A, 4 + 2 * (GROUPS - 1))
            with pe.Fori(0, GROUPS) as g:
                fill = FILL_B + FILLS_B * g
                for n in range(PAIRS):
                    final(n, fill, 2 * (GROUPS - 1) + 2 * g)
                    gemm_pair(C_B + 4 * g, n, 0)
                for j in range(2):
                    for n in range(PAIRS):
                        if n in (4, 5):
                            rotated(n - 4, 12 + 2 * j + n - 4 + 4 * g, FILL_B + 2 + 2 * j + n - 4 + FILLS_B * g)
                        gemm_pair(C_B + 1 + j + 4 * g, n, (j + 1) % 2)
                for n in range(PAIRS):
                    attention_b(n, FILL_B + 6 + FILLS_B * g, UNIT_B + UNITS_B * g)
                    gemm_pair(C_B + 3 + 4 * g, n, 1)
            for n in range(PAIRS):
                final(n, FILL_LAST, 4 * GROUPS - 2)
                gemm_pair(C_OUT, n, 0, ready=mix_ready_pairs)
            with pe.Fori(0, (N_OUT - 2) // 2) as i:
                for j in range(2):
                    for n in range(PAIRS):
                        gemm_pair(C_OUT + 1 + j + 2 * i, n, (j + 1) % 2)
            for n in range(PAIRS - SPLIT_SLOTS):
                gemm_pair(C_OUT + N_OUT - 1, n, 1)
            for t in range(TILES):
                for n in range(PAIRS - SPLIT_SLOTS, PAIRS):
                    gemm_pair(C_OUT + N_OUT - 1, n, 1, tiles=(t,))

        @block.scalar
        def _(act):
            act.dma_start(norm_w[:, :], norm_cols).then_inc(norm_landed, 16)
            a, b = XT_PIECES[0]
            act.dma_start(xt_raw[:, a:b, :], xt_v[:, a:b, :]).then_inc(xt_landed[0], 16)
            act.wait_ge(zeros_ready, 2)
            nc.scalar.activation(stat[:, 6, :], stat[:, 5, :], ACT.Copy)
            act.wait_ge(norm_landed, 16)

            def split(c, n, width=NC):
                act.wait_ge(raw_landed[n % RAW_SLOTS], 16 * (PAIRS // RAW_SLOTS * c + n // RAW_SLOTS + 1))
                if lag(16 * c + n - SPLIT_SLOTS + 1):
                    act.wait_ge(weights_used, 16 * c + (n - SPLIT_SLOTS + 1))
                nc.scalar.activation(w_hi[:, n % SPLIT_SLOTS, :, 0:width], raw[:, n % RAW_SLOTS, :, 0:width],
                                     ACT.Copy).then_inc(hi_ready, 1)

            def evacuate(c, parity, dst, scale):
                act.wait_ge(weights_used, PAIRS * (c + 1))
                nc.scalar.activation(dst, acc[:, parity, 0, :], ACT.Copy, scale=scale).then_inc(acc0_free, 1)

            def take_fill(fill, dst, src=None, scale=1.0):
                act.wait_ge(tr_done, fill + 1)
                src = trans[:, :].rearrange("p (h t) -> p h t", h=HPG) if src is None else src
                nc.scalar.activation(dst, src, ACT.Copy, scale=scale).then_inc(tr_free, 1)

            def exp_unit(u, slot, unit):
                t, h0, nh = UNITS[u]
                nk = P * (t + 1)
                act.wait_ge(max_ready, unit + 1)
                for i in range(nh):
                    p = probs[:, slot, i * nk:(i + 1) * nk]
                    last = nc.scalar.activation(p, p, ACT.Exp, bias=negmax[:, slot, i:i + 1],
                                                accum_out=den[:, slot, i:i + 1])
                last.then_inc(exp_done, 1)

            def exp_z(t, c, tile_no):
                act.wait_ge(acc0_free if t == 0 else acc1_free, c)
                nc.scalar.activation(mixed[:, t, :], tok_b[:, t, :], ACT.Exp, scale=-1.0).then_inc(ez_ready, 1)

            r0, rq0 = scl[:, 0, 0:1], scl[:, 1, 0:1]

            def x_block(n):
                for k in (2 * n, 2 * n + 1):
                    act.wait_ge(xt_landed[[i for i, (a, b) in enumerate(XT_PIECES) if a <= k < b][0]], 16)
                    nc.scalar.activation(x_hi[:, k, :], xt_raw[:, k, :], ACT.Copy, scale=norm_w[:, k:k + 1]
                                         ).then_inc(xhi_ready, 1)

            for n in range(PAIRS + LEAD):
                if n < PAIRS:
                    x_block(n)
                split(C_KSL, n)
                if n == PAIRS + 2:
                    act.wait_ge(angles_ready, 1)
                    nc.scalar.activation(trig[:, :, :, :], trig[:, :, :, :], ACT.Sin).then_inc(trig_ready, 1)
            act.wait_ge(var_ready, 1)
            nc.scalar.activation(stat[:, 2, :], stat[:, 1, :], ACT.Sqrt).then_inc(root_done, 1)
            act.wait_ge(stats_ready, 1)
            evacuate(C_KSL, 1, tok_b[:, 0, :], r0)
            with act.Fori(0, 2) as i:
                for n in range(LEAD, PAIRS + LEAD):
                    split(C_LOOP1 + 2 * i, n)
                evacuate(C_LOOP1 + 2 * i, 0, tok_a[:, 0, :], r0)
                for n in range(LEAD, PAIRS + LEAD):
                    split(C_LOOP1 + 1 + 2 * i, n)
            for n in range(LEAD, PAIRS + LEAD):
                if n - LEAD in (4, 5):
                    t = n - LEAD - 4
                    take_fill(FILL_KSL + t, k_t[:, 0, :, t * P:(t + 1) * P])
                split(C_KW, n)
                if n == LEAD + 1:
                    act.wait_ge(gate_landed, 16)
                    nc.scalar.activation(gate_w[:, :, 0:N_GATE], gate_raw[:, :, :], ACT.Copy).then_inc(gatew_step, 1)
            evacuate(C_KW, 0, tok_a[:, 0, :], r0)
            for n in range(LEAD, PAIRS + LEAD):
                if n - LEAD in (7, 8):
                    t = n - LEAD - 7
                    take_fill(FILL_KW + t, k_t[:, 1, :, t * P:(t + 1) * P])
                split(C_CMP, n)
                if n == LEAD + 5:
                    act.wait_ge(tr_free, FILL_GATE + 1)
                    nc.scalar.activation(gates[:, :, :, :], gates[:, :, :, :], ACT.Exp, scale=-1.0
                                         ).then_inc(gate_exp, 1)
            for n in range(LEAD, PAIRS + LEAD):
                if n - LEAD == 2:
                    act.wait_ge(gelu_step, 3)
                    nc.scalar.activation(gelu[:, :], gelu[:, :], ACT.Tanh, scale=math.sqrt(2 / math.pi)
                                         ).then_inc(tanh_done, 1)
                if n - LEAD == 5:
                    take_fill(FILL_CMP, hid_t[:, :, :], trans[:, 0:2 * P].rearrange("p (j r) -> p j r", j=2), 0.5)
                if n - LEAD == 6:
                    take_fill(FILL_CMP + 1, kc_t[:, :], trans[:, 0:64])
                if n - LEAD == 7:
                    take_fill(FILL_CMP + 2, vc[:, :, :], trans[0:CMP_PAD, :].rearrange("p (h d) -> p h d", h=GROUPS))
                split(C_QA0, n)
            evacuate(C_QA0, 0, tok_a[:, 0, :], rq0)

            def attention_a_frame(c, fill, unit):
                for n in range(LEAD, PAIRS + LEAD):
                    at = n - LEAD
                    if at in (1, 2):
                        take_fill(fill + at - 1, qraw_t[:, :, (at - 1) * P:at * P])
                    if at in (4, 5):
                        take_fill(fill + at - 2, qrot_t[:, :, (at - 4) * P:(at - 3) * P])
                    if at in (6, 7):
                        take_fill(fill + at - 2, probs_t[0:CMP_PAD, at - 6, :], trans[0:CMP_PAD, :])
                    if 9 <= at <= 14:
                        take_fill(fill + at - 3, probs_t[:, (at - 9) % 2, :], trans[:, :])
                    split(c, n)
                    if at == 3:
                        act.wait_ge(max_ready, unit + 1)
                        nc.scalar.activation(probs_c[:, :, :, :], probs_c[:, :, :, :], ACT.Exp).then_inc(exp_done, 1)
                    if 6 <= at <= 11:
                        exp_unit((at - 6) % 3, (at - 6) % 4, unit + 1 + at - 6)

            def mixing_frame(c, tiles_mixed):
                evacuate(c - 1, 1, tok_b[:, 0, :], r0)
                for n in range(LEAD, PAIRS + LEAD):
                    split(c, n)
                    if n - LEAD in (0, 1):
                        exp_z(n - LEAD, c, tiles_mixed + n - LEAD)
                evacuate(c, 0, tok_a[:, 0, :], rq0)

            with act.Fori(0, GROUPS - 1) as g:
                per = FILLS_A + FILLS_FINAL
                attention_a_frame(C_A + 2 * g, FILL_A + per * g, UNITS_A * g)
                mixing_frame(C_A + 1 + 2 * g, 2 * g)
            attention_a_frame(C_B - 1, FILL_B - FILLS_A, UNIT_B - UNITS_A)
            with act.Fori(0, GROUPS) as g:
                mixing_frame(C_B + 4 * g, 2 * (GROUPS - 1) + 2 * g)
                for j in range(2):
                    for n in range(LEAD, PAIRS + LEAD):
                        if n - LEAD in (4, 5):
                            t = n - LEAD - 4
                            dst = qrot_t if j == 0 else k_t[:, 0, :, :]
                            take_fill(FILL_B + 2 + 2 * j + t + FILLS_B * g, dst[:, :, t * P:(t + 1) * P])
                        split(C_B + 1 + j + 4 * g, n)
                    evacuate(C_B + 1 + j + 4 * g, (j + 1) % 2, tok_a[:, 0, :] if j == 0 else v_tok[:, 0, 0, :], r0)
                for n in range(LEAD, PAIRS + LEAD):
                    at = n - LEAD
                    if at in (4, 6, 8):
                        u = (at - 4) // 2
                        take_fill(FILL_B + 6 + u + FILLS_B * g, probs_t[:, u % 2, :], trans[:, :])
                    split(C_B + 3 + 4 * g, n)
                    if at in (1, 3, 5):
                        u = (at - 1) // 2
                        exp_unit(u, u, UNIT_B + u + UNITS_B * g)

            def square(n, parity):
                act.wait_ge(weights_used, PAIRS * (C_OUT + n + 1))
                act.wait_ge(acc1_free, C_OUT + n)
                nc.scalar.activation(junk[:, :], acc[:, parity, 0, :], ACT.Square, accum_out=ssq[:, parity, 0:1]
                                     ).then_inc(y_square, 1)
                act.wait_ge(y_scaled, n + 1)
                act.wait_ge(y_square, n + 1)
                nc.scalar.activation(junk[:, :], acc[:, parity, 1, :], ACT.Square, accum_out=ssq[:, parity, 1:2]
                                     ).then_inc(acc1_free, 1)

            def mix_block(n):
                act.wait_ge(weights_used, PAIRS * (C_OUT - 1) + n + 1)
                act.wait_ge(tr_free, FILL_LAST + (2 if n >= PAIRS - 2 else 0))
                nc.scalar.activation(x_hi[:, 2 * n:2 * n + 2, :], mix_t[:, 2 * n:2 * n + 2, :], ACT.Copy
                                     ).then_inc(mixhi_ready, 1)

            for n in range(LEAD):
                mix_block(n)
            evacuate(C_OUT - 1, 1, tok_b[:, 0, :], r0)
            for n in range(LEAD, PAIRS + LEAD):
                if n < PAIRS:
                    mix_block(n)
                split(C_OUT, n)
                if n - LEAD in (0, 1):
                    exp_z(n - LEAD, C_OUT, 4 * GROUPS - 2 + n - LEAD)
            square(0, 0)
            with act.Fori(0, (N_OUT - 2) // 2) as i:
                for j in range(2):
                    for n in range(LEAD, PAIRS + LEAD):
                        split(C_OUT + 1 + j + 2 * i, n)
                    square(1 + j + 2 * i, (j + 1) % 2)
            nc.scalar.activation(stat[:, 5, :], stat[:, 1, :], ACT.Sqrt)
            for n in range(LEAD, PAIRS):
                split(C_OUT + N_OUT - 1, n)
            act.wait_ge(acc1_free, C_OUT + N_OUT - 1)
            for t in range(TILES):
                if t == 0:
                    act.wait_ge(last_tile0, 1)
                else:
                    act.wait_ge(weights_used, PAIRS * (C_OUT + N_OUT))
                    act.wait_ge(y_square, N_OUT)
                nc.scalar.activation(junk[:, :], acc[:, 1, t, :], ACT.Square, accum_out=ssq[:, 1, t:t + 1]
                                     ).then_inc(y_square, 1)
                act.wait_ge(var_ready, 2 + t)
                nc.scalar.activation(stat[:, 2, t:t + 1], stat[:, 1, t:t + 1], ACT.Sqrt).then_inc(root_done, 1)
                act.wait_ge(final_ready, 1 + t)
                for piece in POOL_PIECES:
                    if OUT_PIECES[piece][0] == t:
                        c = OUT_PIECES[piece][1]
                        nc.scalar.activation(y[:, t, c:c + OUT_COLS], y[:, t, c:c + OUT_COLS], ACT.Copy,
                                             scale=scl[:, 0, t:t + 1]).then_inc(y_rescaled, 1)

        @block.vector
        def _(dve):
            V = nc.vector
            links = [0]

            def link(ins):
                links[0] += 1
                ins.then_inc(chain, 1)
                dve.wait_ge(chain, links[0])

            def split(c, n, width=NC):
                dve.wait_ge(hi_ready, 16 * c + n + 1)
                s = n % SPLIT_SLOTS
                V.tensor_tensor(w_lo[:, s, :, 0:width], raw[:, n % RAW_SLOTS, :, 0:width],
                                w_hi[:, s, :, 0:width].bitcast(F32), ALU.subtract).then_inc(lo_ready, 1)

            def evacuate(c, parity, dst, scale, t=1):
                dve.wait_ge(weights_used, PAIRS * (c + 1))
                V.tensor_scalar(dst, acc[:, parity, t, :], scale, None, ALU.mult
                                ).then_inc(acc0_free if t == 0 else acc1_free, 1)

            def take_fill(fill, dst):
                dve.wait_ge(tr_done, fill + 1)
                V.tensor_scalar(dst, trans[:, :].rearrange("p (h t) -> p h t", h=HPG), 1.0, None, ALU.mult
                                ).then_inc(tr_free, 1)

            def variance(sums, t=slice(0, TILES)):
                V.tensor_scalar(stat[:, 1, t], sums, 1.0 / D_MODEL, EPS, ALU.mult, ALU.add
                                ).then_inc(var_ready, 1)

            def inverse_rms(which, then, count=1, t=slice(0, TILES)):
                dve.wait_ge(root_done, which)
                link(V.reciprocal(stat[:, 3, t], stat[:, 2, t]))
                link(V.tensor_tensor(stat[:, 4, t], stat[:, 3, t], stat[:, 3, t], ALU.mult))
                link(V.scalar_tensor_tensor(stat[:, 4, t], stat[:, 4, t], -0.5, stat[:, 1, t], ALU.mult, ALU.mult))
                V.scalar_tensor_tensor(scl[:, 0, t], stat[:, 4, t], 1.5, stat[:, 3, t], ALU.add, ALU.mult
                                       ).then_inc(then, 1)
                dve.wait_ge(then, count)

            r = [scl[:, 0, t:t + 1] for t in range(TILES)]
            rq1 = scl[:, 1, 1:2]

            def x_rest(n):
                for k in (2 * n, 2 * n + 1):
                    dve.wait_ge(xhi_ready, k + 1)
                    last = V.scalar_tensor_tensor(x_lo[:, k, :], xt_raw[:, k, :], norm_w[:, k:k + 1],
                                                  x_hi[:, k, :].bitcast(F32), ALU.mult, ALU.subtract)
                last.then_inc(x_ready, 1)

            turn_parts, rest = [], 2 * math.pi
            for bits in (5, 14, 23):
                turn_parts.append(round(rest * 2 ** bits) / 2 ** bits)
                rest -= turn_parts[-1]
            turn_parts.append(rest)

            def angles(step):
                if step == 0:
                    link(V.tensor_copy(pos_f[:, :], pos_i[:, :]))
                if step in (1, 2):
                    for t in range(TILES):
                        link(V.tensor_scalar(trig[:, step - 1, t, :], inv_freq, pos_f[:, t:t + 1], None, ALU.mult))
                if step == 3:
                    link(V.tensor_scalar(turns[:, 0, :, :], trig[:, 0, :, :], 1 / (2 * math.pi), None, ALU.mult))
                    link(V.tensor_scalar(turns[:, 1, :, :], trig[:, 1, :, :], 1 / (2 * math.pi), 0.25,
                                         ALU.mult, ALU.add))
                if step == 4:
                    link(V.tensor_scalar(turns[:, :, :, :], turns[:, :, :, :], 1.5 * 2 ** 23, None, ALU.add))
                    link(V.tensor_scalar(turns[:, :, :, :], turns[:, :, :, :], 1.5 * 2 ** 23, None, ALU.subtract))
                if step in (5, 6, 7, 8):
                    link(V.scalar_tensor_tensor(trig[:, :, :, :], turns[:, :, :, :], -turn_parts[step - 5],
                                                trig[:, :, :, :], ALU.mult, ALU.add))
                if step == 9:
                    link(V.tensor_scalar(trig[:, 1, :, :], trig[:, 1, :, :], math.pi / 2, None, ALU.add))
                    V.tensor_scalar(trig[:, :, :, :], trig[:, :, :, :], 3.1415925, -3.1415925, ALU.min, ALU.max
                                    ).then_inc(angles_ready, 1)

            V.memset(hidden[:, :], 0.0).then_inc(zeros_ready, 1)
            V.memset(stat[:, 5, :], 0.0).then_inc(zeros_ready, 1)
            dve.wait_ge(norm_landed, 16)
            for n in range(PAIRS + LEAD):
                if n < PAIRS:
                    x_rest(n)
                split(C_KSL, n)
                if n == 8:
                    dve.wait_ge(consts_landed, 16 * 2)
                angles(n - 8)
            dve.wait_ge(sumsq_done, 1)
            variance(trans[:, 0:TILES])
            inverse_rms(1, rms_ready)
            V.tensor_scalar(scl[:, 1, :], scl[:, 0, :], SCALE, None, ALU.mult).then_inc(stats_ready, 1)
            dve.wait_ge(stats_ready, 1)
            evacuate(C_KSL, 1, tok_b[:, 1, :], r[1])
            dve.wait_ge(flat_zeroed, 2)

            with dve.Fori(0, 2) as i:
                for n in range(LEAD, PAIRS + LEAD):
                    split(C_LOOP1 + 2 * i, n)
                evacuate(C_LOOP1 + 2 * i, 0, tok_a[:, 1, :], r[1])
                for n in range(LEAD, PAIRS + LEAD):
                    split(C_LOOP1 + 1 + 2 * i, n)
                    at = n - LEAD
                    if at in (1, 2):
                        take_fill(2 * i + at - 1, k_t[:, i, :, (at - 1) * P:at * P])
                    if at in (4, 5):
                        a = at - 4
                        dve.wait_ge(tr_free, 2 * i + 2)
                        src = k_t[:, i, :, :].rearrange("p h (c b) -> p h c b", b=CMP_STRIDE)[:, :, a:a + N_CMP, :]
                        pe_row = pe_t[:, i, a, :].unsqueeze(1).unsqueeze(1).broadcast_to([P, HPG, N_CMP, CMP_STRIDE])
                        V.tensor_tensor(blocks[:, a, :, :, :], src, pe_row, ALU.add).then_inc(flat_step, 1)
                    if at in (6, 7, 8, 9):
                        a = at % 2
                        half = [f[:, a * CMP_STRIDE:(a + 1) * CMP_STRIDE, :].rearrange(
                            "p b (v h c) -> p v h c b", v=2, h=HPG)[:, i, :, 0:N_CMP, :] for f in (flat_hi, flat_lo)]
                        if at < 8:
                            dve.wait_ge(flat_step, 6 * i + a + 1)
                            V.tensor_scalar(half[0], blocks[:, a, :, :, :], 1.0, None, ALU.mult).then_inc(flat_step, 1)
                        else:
                            dve.wait_ge(flat_step, 6 * i + 3 + a)
                            V.tensor_tensor(half[1], blocks[:, a, :, :, :], half[0].bitcast(F32), ALU.subtract
                                            ).then_inc(flat_step, 1)
                for t in range(TILES):
                    evacuate(C_LOOP1 + 1 + 2 * i, 1, v_tok[:, i, t, :], r[t], t)
            for n in range(LEAD, PAIRS + LEAD):
                split(C_KW, n)
                if n == LEAD + 2:
                    dve.wait_ge(gatew_step, 1)
                    V.tensor_tensor(gate_w[:, :, N_GATE:2 * N_GATE], gate_raw[:, :, :],
                                    gate_w[:, :, 0:N_GATE].bitcast(F32), ALU.subtract).then_inc(gatew_step, 1)
                if n == LEAD + 10:
                    dve.wait_ge(gate_done, 1)
                    V.tensor_copy(gate_sum, scores[0:2 * N_GATE, 0:SEQ]).then_inc(gate_moved, 1)
                    dve.wait_ge(gate_moved, 1)
                    V.tensor_tensor(gate_sum, gate_sum, scores[0:2 * N_GATE, SEQ:2 * SEQ], ALU.add
                                    ).then_inc(gate_moved, 1)
            evacuate(C_KW, 0, tok_a[:, 1, :], r[1])
            for n in range(LEAD, PAIRS + LEAD):
                split(C_CMP, n)
                if n - LEAD == 3:
                    dve.wait_ge(tr_done, FILL_GATE + 1)
                    for t in range(TILES):
                        last = V.scalar_tensor_tensor(gates[:, t, :, :].rearrange("p h b -> p (h b)"),
                                                      trans[:, t * N_GATE:(t + 1) * N_GATE], r[t], b_gate,
                                                      ALU.mult, ALU.add)
                    last.then_inc(tr_free, 1)
                if n - LEAD == 7:
                    dve.wait_ge(gate_exp, 1)
                    link(V.tensor_scalar(gates[:, :, :, :], gates[:, :, :, :], 1.0, None, ALU.add))
                    link(V.reciprocal(gates[:, :, :, :], gates[:, :, :, :]))
                    for t in range(TILES):
                        link(V.tensor_scalar(gates[:, t, :, 0], gates[:, t, :, 0], any_cmp[:, t:t + 1], None, ALU.mult))
            dve.wait_ge(weights_used, PAIRS * (C_CMP + 1))
            for v in range(2):
                rows, cols = slice(64 * v, 64 * v + 64), slice(CMP_HIDDEN * v, CMP_HIDDEN * (v + 1))
                V.tensor_copy(hidden[rows, :], acc[rows, 1, 0, cols]).then_inc(acc0_free if v == 0 else acc1_free, 1)
            for n in range(LEAD, PAIRS + LEAD):
                split(C_QA0, n)
                if n == LEAD:
                    dve.wait_ge(acc0_free, C_CMP + 1)
                    dve.wait_ge(acc1_free, C_CMP + 1)
                    V.tensor_tensor(gelu[:, :], hidden[:, :], hidden[:, :], ALU.mult).then_inc(gelu_step, 1)
                    dve.wait_ge(gelu_step, 1)
                    V.tensor_scalar(gelu[:, :], gelu[:, :], 0.044715, 1.0, ALU.mult, ALU.add).then_inc(gelu_step, 1)
                    dve.wait_ge(gelu_step, 2)
                    V.tensor_tensor(gelu[:, :], gelu[:, :], hidden[:, :], ALU.mult).then_inc(gelu_step, 1)
                if n == LEAD + 3:
                    dve.wait_ge(tanh_done, 1)
                    V.scalar_tensor_tensor(gelu[:, :], gelu[:, :], 1.0, hidden[:, :], ALU.add, ALU.mult
                                           ).then_inc(gelu_ready, 1)
            evacuate(C_QA0, 0, tok_a[:, 1, :], rq1)

            def mask_unit(u, slot, unit, bias):
                t, h0, nh = UNITS[u]
                nk = P * (t + 1)
                b = (bias[:, 0:P] if t == 0 else bias[:, P:3 * P]).unsqueeze(1).broadcast_to([P, nh, nk])
                p = probs[:, slot, :].rearrange("p (h n) -> p h n", h=nh)
                dve.wait_ge(scores_done, unit + 1)
                V.tensor_tensor(p, scores[:, :].rearrange("p (h n) -> p h n", h=nh), b, ALU.add
                                ).then_inc(scores_free, 1)
                dve.wait_ge(scores_free, unit + 1)
                V.tensor_reduce(negmax[:, slot, 0:nh], p, AX.X, ALU.max, negate=True).then_inc(max_ready, 1)

            def normalise_unit(u, slot, unit, recips, weights=None, gate=None):
                t, h0, nh = UNITS[u]
                nk = P * (t + 1)
                p = probs[:, slot, :].rearrange("p (h n) -> p h n", h=nh)
                f = rden[:, slot, 0:nh]
                dve.wait_ge(exp_done, unit + 1)
                V.reciprocal(f, den[:, slot, 0:nh]).then_inc(recip_done, 1)
                dve.wait_ge(recip_done, recips + 1)
                if gate is not None:
                    V.tensor_tensor(weight[:, slot, 0:nh], f, gate, ALU.mult).then_inc(weight_done, 1)
                    f = weight[:, slot, 0:nh]
                    dve.wait_ge(weight_done, weights + 1)
                V.tensor_tensor(p, p, f.unsqueeze(2).broadcast_to([P, nh, nk]), ALU.mult).then_inc(probs_ready, 1)

            def attention_a_frame(c, g, unit):
                for n in range(LEAD, PAIRS + LEAD):
                    at = n - LEAD
                    if at == 3:
                        view = scores[:, 0:TILES * HPG * CMP_PAD].rearrange("p (t h c) -> p t h c", t=TILES, h=HPG)
                        dve.wait_ge(scores_done, unit + 1)
                        for t in range(TILES):
                            last = V.tensor_tensor(probs_c[:, t, :, :], view[:, t, :, :],
                                                   cmp_bias[:, t, :].unsqueeze(1).broadcast_to([P, HPG, CMP_PAD]),
                                                   ALU.add)
                        last.then_inc(scores_free, 1)
                        dve.wait_ge(scores_free, unit + 1)
                        V.tensor_reduce(cstat[:, 0, :, :], probs_c[:, :, :, :], AX.X, ALU.max, negate=True
                                        ).then_inc(cmp_step, 1)
                        dve.wait_ge(cmp_step, 4 * g + 1)
                        V.tensor_tensor(probs_c[:, :, :, :], probs_c[:, :, :, :],
                                        cstat[:, 0, :, :].unsqueeze(3).broadcast_to([P, TILES, HPG, CMP_PAD]), ALU.add
                                        ).then_inc(max_ready, 1)
                    if 6 <= at <= 11:
                        u = at - 6
                        mask_unit(u % 3, u % 4, unit + 1 + u, causal)
                    split(c, n)
                    if at == 4:
                        dve.wait_ge(exp_done, unit + 1)
                        V.tensor_reduce(cstat[:, 1, :, :], probs_c[:, :, :, :], AX.X, ALU.add).then_inc(cmp_step, 1)
                        dve.wait_ge(cmp_step, 4 * g + 2)
                        V.reciprocal(cstat[:, 2, :, :], cstat[:, 1, :, :]).then_inc(cmp_step, 1)
                        dve.wait_ge(cmp_step, 4 * g + 3)
                        V.tensor_tensor(cstat[:, 3, :, :], cstat[:, 2, :, :], gates[:, :, bass.ds(HPG * g, HPG), 0],
                                        ALU.mult).then_inc(cmp_step, 1)
                        dve.wait_ge(cmp_step, 4 * g + 4)
                        V.tensor_tensor(probs_c[:, :, :, :], probs_c[:, :, :, :],
                                        cstat[:, 3, :, :].unsqueeze(3).broadcast_to([P, TILES, HPG, CMP_PAD]),
                                        ALU.mult).then_inc(probs_ready, 1)
                    if 7 <= at <= 12:
                        u = at - 7
                        t, h0, nh = UNITS[u % 3]
                        normalise_unit(u % 3, u % 4, unit + 1 + u, 6 * g + u, 6 * g + u,
                                       gates[:, t, bass.ds(HPG * g + h0, nh), 1 + u // 3])

            def mix_tile(at, group):
                if at not in (1, 2, 3, 4, 5, 6):
                    return
                t, step = (at - 1) // 3, (at - 1) % 3
                base = 8 * group + 4 * t
                m = mixed[:, t, :]
                if step == 0:
                    dve.wait_ge(ez_ready, 2 * group + t + 1)
                    V.tensor_scalar(m, m, 1.0, None, ALU.add).then_inc(silu_step, 1)
                    dve.wait_ge(silu_step, base + 1)
                if step < 2:
                    half = m[:, step * 256:(step + 1) * 256]
                    V.reciprocal(half, half).then_inc(silu_step, 1)
                else:
                    dve.wait_ge(silu_step, base + 3)
                    V.tensor_tensor(m, m, tok_b[:, t, :], ALU.mult).then_inc(silu_step, 1)
                    dve.wait_ge(silu_step, base + 4)
                    dve.wait_ge(heads_done, group + 1)
                    V.tensor_tensor(m, m, heads[:, t, :], ALU.mult).then_inc(mix_ready, 1)

            def store_mixed(at, group, fill):
                if at in (6, 10):
                    t = (at - 6) // 4
                    take_fill(fill + t, mix_t[:, bass.ds(HPG * group, HPG), t * P:(t + 1) * P])

            def mixing_frame(c, group, fill):
                evacuate(c - 1, 1, tok_b[:, 1, :], r[1])
                for n in range(LEAD, PAIRS + LEAD):
                    store_mixed(n - LEAD, group, fill)
                    split(c, n)
                    mix_tile(n - LEAD, group)
                evacuate(c, 0, tok_a[:, 1, :], rq1)

            with dve.Fori(0, GROUPS - 1) as g:
                attention_a_frame(C_A + 2 * g, g, UNITS_A * g)
                mixing_frame(C_A + 1 + 2 * g, g, FILL_A + FILLS_A + (FILLS_A + FILLS_FINAL) * g)
            attention_a_frame(C_B - 1, GROUPS - 1, UNIT_B - UNITS_A)
            with dve.Fori(0, GROUPS) as g:
                mixing_frame(C_B + 4 * g, GROUPS - 1 + g, FILL_B + FILLS_B * g)
                for j in range(2):
                    for n in range(LEAD, PAIRS + LEAD):
                        split(C_B + 1 + j + 4 * g, n)
                    evacuate(C_B + 1 + j + 4 * g, (j + 1) % 2, tok_a[:, 1, :] if j == 0 else v_tok[:, 0, 1, :], r[1])
                for n in range(LEAD, PAIRS + LEAD):
                    at = n - LEAD
                    if at in (1, 3, 5):
                        u = (at - 1) // 2
                        mask_unit(u, u, UNIT_B + u + UNITS_B * g, dilated)
                    split(C_B + 3 + 4 * g, n)
                    if at in (2, 4, 6):
                        u = (at - 2) // 2
                        normalise_unit(u, u, UNIT_B + u + UNITS_B * g, 6 * GROUPS + u + UNITS_B * g)

            def scale_chunk(n, parity, cols, uses):
                dve.wait_ge(weights_used, PAIRS * (C_OUT + n + 1))
                dve.wait_ge(wpost_landed[parity], 16 * uses)
                V.tensor_tensor(y[:, 1, cols], acc[:, parity, 1, :], wpost[:, parity, :], ALU.mult).then_inc(y_scaled, 1)
                dve.wait_ge(y_square, n + 1)
                V.tensor_tensor(y[:, 0, cols], acc[:, parity, 0, :], wpost[:, parity, :], ALU.mult).then_inc(acc0_free, 1)
                dve.wait_ge(acc1_free, C_OUT + n + 1)

            def mix_rest(n):
                dve.wait_ge(mixhi_ready, n + 1)
                V.tensor_tensor(x_lo[:, 2 * n:2 * n + 2, :], mix_t[:, 2 * n:2 * n + 2, :],
                                x_hi[:, 2 * n:2 * n + 2, :].bitcast(F32), ALU.subtract).then_inc(mix_ready_pairs, 1)

            for n in range(LEAD):
                mix_rest(n)
            evacuate(C_OUT - 1, 1, tok_b[:, 1, :], r[1])
            for n in range(LEAD, PAIRS + LEAD):
                store_mixed(n - LEAD, 2 * GROUPS - 1, FILL_LAST)
                if n < PAIRS:
                    mix_rest(n)
                split(C_OUT, n)
                mix_tile(n - LEAD, 2 * GROUPS - 1)
            scale_chunk(0, 0, slice(0, NC), 1)
            V.tensor_copy(ssum[:, :], ssq[:, 0, :]).then_inc(ssum_done, 1)
            with dve.Fori(0, (N_OUT - 2) // 2) as i:
                for j in range(2):
                    for n in range(LEAD, PAIRS + LEAD):
                        split(C_OUT + 1 + j + 2 * i, n)
                    scale_chunk(1 + j + 2 * i, (j + 1) % 2, bass.ds(NC * (1 + j) + 2 * NC * i, NC),
                                1 + j + i)
                    dve.wait_ge(ssum_done, 1 + j + 2 * i)
                    V.tensor_tensor(ssum[:, :], ssum[:, :], ssq[:, (j + 1) % 2, :], ALU.add).then_inc(ssum_done, 1)
            for n in range(LEAD, PAIRS):
                split(C_OUT + N_OUT - 1, n)
            last_cols = slice(NC * (N_OUT - 1), NC * N_OUT)
            dve.wait_ge(wpost_landed[1], 16 * (N_OUT // 2))
            dve.wait_ge(xres_landed, 16 * TILES * N_OUT)
            dve.wait_ge(ssum_done, N_OUT - 1)
            for t in range(TILES):
                one = slice(t, t + 1)
                dve.wait_ge(y_square, N_OUT + t)
                link(V.tensor_tensor(stat[:, 0, one], ssum[:, one], ssq[:, 1, one], ALU.add))
                variance(stat[:, 0, one], one)
                V.tensor_tensor(y[:, t, last_cols], acc[:, 1, t, :], wpost[:, 1, :], ALU.mult).then_inc(y_scaled, 1)
                inverse_rms(2 + t, final_ready, 1 + t, one)
                dve.wait_ge(y_scaled, N_OUT + t)
                for i, (tile, c) in enumerate(OUT_PIECES):
                    if tile == t and i not in POOL_PIECES:
                        V.scalar_tensor_tensor(y[:, t, c:c + OUT_COLS], y[:, t, c:c + OUT_COLS], r[t],
                                               x_tok[:, t, c:c + OUT_COLS], ALU.mult, ALU.add).then_inc(y_added, 1)


def constants():
    i, j = np.arange(SEQ)[:, None], np.arange(SEQ)[None, :]
    dist = i - j
    causal = np.where(dist >= 0, 0.0, NEG)
    seen = sum(((dist >= 0) & (dist % d == 0) & (dist // d <= w // d)).astype(int)
               for w, d in ((128, 1), (512, 4), (2048, 16)))
    dilated = np.where(seen > 0, np.log(np.maximum(seen, 1)), NEG)
    c = np.arange(CMP_PAD)[None, :]
    valid = (c * CMP_STRIDE + CMP_LEN - 1 <= i) & (c < N_CMP)
    cmp_bias = np.where(valid, 0.0, NEG)
    tok = lambda a: a.reshape(TILES, P, -1).transpose(1, 0, 2).reshape(P, -1)
    two = lambda a: np.concatenate([a[:P, :P], a[P:, :]], axis=1)
    half = HEAD // 2
    inv = np.float32(ROPE_THETA) ** (-np.arange(half, dtype=np.float32) / np.float32(half))
    return [np.eye(P), two(causal), two(dilated), tok(cmp_bias), tok(valid.any(axis=1, keepdims=True)),
            np.broadcast_to(inv, (P, half))]


def kernel(x, positions, pre_norm_w, post_norm_w, w_in, b_gate, cmp_pe_k, cmp_pe_v,
           cmp_wk1, cmp_wk2, cmp_wv1, cmp_wv2, w_out):
    import concourse.bacc as bacc
    from concourse.bass_utils import run_bass_kernel_spmd

    f = lambda a: np.asarray(a, dtype=np.float32)
    x = np.ascontiguousarray(f(x)[0])
    pe = np.stack([f(cmp_pe_k)[0].T, f(cmp_pe_v)[0].T], axis=1).reshape(P, 2 * CMP_LEN)
    table = np.concatenate([a.astype(np.float32) for a in constants()] + [
        pe, np.broadcast_to(f(b_gate)[0], (P, N_GATE)), np.ones((P, 1), np.float32)], axis=1)
    arrays = {
        "in_x": x,
        "in_x_t": np.ascontiguousarray(x.T),
        "in_positions": np.ascontiguousarray(np.asarray(positions, dtype=np.int32)[0].reshape(TILES, P).T),
        "in_norm": np.ascontiguousarray(f(pre_norm_w)[0].reshape(KB, P).T),
        "in_table": np.ascontiguousarray(table),
        "in_w_in": np.ascontiguousarray(f(w_in)[0]),
        "in_w1": np.concatenate([f(cmp_wk1)[0], f(cmp_wv1)[0]], axis=1),
        "in_w2": np.ascontiguousarray(np.stack([f(cmp_wk2)[0], f(cmp_wv2)[0]]).reshape(2, 2, P, P).transpose(2, 0, 1, 3)),
        "in_post_w": np.ascontiguousarray(f(post_norm_w)),
        "in_w_out": np.ascontiguousarray(f(w_out)[0]),
    }
    nc = bacc.Bacc("TRN2", target_bir_lowering=False, num_devices=1, dynamic_dma_scratch_size=1024)
    t = {n: nc.dram_tensor(n, a.shape, mybir.dt.from_np(a.dtype), kind="ExternalInput").ap()
         for n, a in arrays.items()}
    out = nc.dram_tensor("out_0", (SEQ, D_MODEL), F32, kind="ExternalOutput").ap()
    build(nc, t["in_x"], t["in_x_t"], t["in_positions"], t["in_norm"], t["in_table"], t["in_w_in"], t["in_w1"], t["in_w2"],
          t["in_post_w"], t["in_w_out"], out)
    r = run_bass_kernel_spmd(nc, [arrays], core_ids=[0])
    return r.results[0]["out_0"].reshape(1, SEQ, D_MODEL)
```
